# Optimizing a Trainium2 kernel written in Bass

```python
import jax, jax.numpy as jnp
from jax import lax
import numpy as np

D_MODEL = 2048
BATCH = 1
SEQ = 256
DEPTH = 1
DEC_BATCH = 8
DEC_SEQ = 8
PAST_LEN = 256
PAGE_SIZE = 128

H_A = 8
DH_A = D_MODEL // 16
W_A = H_A * DH_A
H_R = 8
DK_R = D_MODEL // 16
DV_R = D_MODEL // 16
W_R = H_R * DV_R
D_FF = ((8 * D_MODEL // 3 + 255) // 256) * 256
CONV_W = 3
Q_BLOCK = 128
RET_CHUNK = 128
ROPE_BASE = 10000.0
LN_EPS = 1e-5
GN_EPS = 1e-5
ALPHA = (2.0 * DEPTH) ** 0.25
BETA = (8.0 * DEPTH) ** -0.25
IN_SIZES = (W_A, W_A, W_A, H_A, H_R * DK_R, H_R * DK_R, W_R, W_R, D_MODEL, D_MODEL)
N_IN = sum(IN_SIZES)

kernel_name = 'hybrid_fox_retnet_convffn_step'

def _ln(x, g, b):
    xf = x.astype(jnp.float32)
    mu = jnp.mean(xf, -1, keepdims=True)
    var = jnp.mean(jnp.square(xf - mu), -1, keepdims=True)
    y = (xf - mu) * lax.rsqrt(var + LN_EPS) * g.astype(jnp.float32) + b.astype(jnp.float32)
    return y.astype(x.dtype)

def _rope(x, pos):
    half = x.shape[-1] // 2
    inv = ROPE_BASE ** (-jnp.arange(half, dtype=jnp.float32) / half)
    ang = pos.astype(jnp.float32)[:, None] * inv[None, :]
    cos = jnp.cos(ang)[None, :, None, :]
    sin = jnp.sin(ang)[None, :, None, :]
    xf = x.astype(jnp.float32)
    x1, x2 = xf[..., :half], xf[..., half:]
    return jnp.concatenate([x1 * cos - x2 * sin, x1 * sin + x2 * cos], -1).astype(x.dtype)

def _fox_attend(q, k, v, cq, ck, q0):
    nq, nk = q.shape[1], k.shape[1]
    s = jnp.einsum('bqhd,bkhd->bhqk', q, k).astype(jnp.float32) * (q.shape[-1] ** -0.5)
    s = s + jnp.transpose(cq, (0, 2, 1))[:, :, :, None] - jnp.transpose(ck, (0, 2, 1))[:, :, None, :]
    causal = (q0 + jnp.arange(nq))[:, None] >= jnp.arange(nk)[None, :]
    p = jax.nn.softmax(jnp.where(causal, s, -jnp.inf), axis=-1)
    return jnp.einsum('bhqk,bkhd->bqhd', p.astype(v.dtype), v)

def _forgetting_attention(q, k, v, logf, past):
    if past is None:
        c = jnp.cumsum(logf, axis=1)
        T = q.shape[1]
        qb = min(Q_BLOCK, T)
        outs = [_fox_attend(q[:, s:s + qb], k[:, :s + qb], v[:, :s + qb], c[:, s:s + qb], c[:, :s + qb], s)
                for s in range(0, T, qb)]
        return jnp.concatenate(outs, axis=1)
    kp, vp, lfp = past
    P = kp.shape[1]
    k_all = jnp.concatenate([kp.astype(k.dtype), k], axis=1)
    v_all = jnp.concatenate([vp.astype(v.dtype), v], axis=1)
    c = jnp.cumsum(jnp.concatenate([lfp.astype(jnp.float32), logf], axis=1), axis=1)
    return _fox_attend(q, k_all, v_all, c[:, P:], c, P)

def _ret_chunk(S, q, k, v, lg):
    C = q.shape[1]
    idx = jnp.arange(C, dtype=jnp.float32)
    diff = idx[:, None] - idx[None, :]
    dmat = jnp.where(diff[None] >= 0, jnp.exp(diff[None] * lg[:, None, None]), 0.0)
    att = jnp.einsum('bihd,bjhd->bhij', q, k) * dmat[None]
    inner = jnp.einsum('bhij,bjhe->bihe', att, v)
    cross = jnp.einsum('bihd,bhde->bihe', q, S) * jnp.exp((idx + 1.0)[:, None] * lg[None, :])[None, :, :, None]
    w_in = jnp.exp((C - 1.0 - idx)[:, None] * lg[None, :])
    S_new = jnp.exp(C * lg)[None, :, None, None] * S + jnp.einsum('bjhd,bjhe,jh->bhde', k, v, w_in)
    return S_new, inner + cross

def _retention(q, k, v, S0):
    lg = jnp.log(1.0 - jnp.exp2(-5.0 - jnp.arange(H_R, dtype=jnp.float32)))
    B, T = q.shape[0], q.shape[1]
    C = RET_CHUNK if T % RET_CHUNK == 0 else T
    n = T // C

    def to_chunks(a):
        return jnp.swapaxes(a.astype(jnp.float32).reshape((B, n, C) + a.shape[2:]), 0, 1)

    def step(S, qkv):
        return _ret_chunk(S, qkv[0], qkv[1], qkv[2], lg)

    S, o = lax.scan(step, S0.astype(jnp.float32), (to_chunks(q), to_chunks(k), to_chunks(v)))
    return jnp.swapaxes(o, 0, 1).reshape(B, T, H_R, DV_R), S

def _layer(x, cond, t0, past, ret_state, conv_state, w_ada, b_ada, w_in, b_f, w_pa, w_pb, w_o,
           ln1_g, ln1_b, w_up, conv_w, conv_b, w_down, ln2_g, ln2_b):
    B, T, _ = x.shape
    mod = jax.nn.silu(cond) @ w_ada + b_ada
    sh1, sc1, g1, sh2, sc2, g2 = [m[:, None, :] for m in jnp.split(mod, 6, axis=-1)]
    u = x * (1 + sc1) + sh1
    proj = u @ w_in
    qa, ka, va, fa, qr, kr, vr, gr, ga, gb = jnp.split(proj, np.cumsum(IN_SIZES)[:-1].tolist(), axis=-1)
    qa = qa.reshape(B, T, H_A, DH_A)
    ka = ka.reshape(B, T, H_A, DH_A)
    va = va.reshape(B, T, H_A, DH_A)
    logf = jax.nn.log_sigmoid(fa.astype(jnp.float32) + b_f.astype(jnp.float32))
    oa = _forgetting_attention(qa, ka, va, logf, past).reshape(B, T, W_A)
    pos = t0 + jnp.arange(T)
    qr = _rope(qr.reshape(B, T, H_R, DK_R), pos)
    kr = _rope(kr.reshape(B, T, H_R, DK_R), pos) * (DK_R ** -0.5)
    orr, ret_new = _retention(qr, kr, vr.reshape(B, T, H_R, DV_R), ret_state)
    mu = jnp.mean(orr, -1, keepdims=True)
    var = jnp.mean(jnp.square(orr - mu), -1, keepdims=True)
    orr = (orr - mu) * lax.rsqrt(var + GN_EPS)
    ob = (orr.reshape(B, T, W_R) * jax.nn.silu(gr.astype(jnp.float32))).astype(x.dtype)
    merged = jax.nn.sigmoid(ga) * (oa @ w_pa) + jax.nn.sigmoid(gb) * (ob @ w_pb)
    x = _ln(ALPHA * x + g1 * (merged @ w_o), ln1_g, ln1_b)
    u2 = x * (1 + sc2) + sh2
    a, bv = jnp.split(u2 @ w_up, 2, axis=-1)
    a_ext = jnp.concatenate([conv_state.astype(a.dtype), a], axis=1)
    conv = conv_b + sum(a_ext[:, w:w + T] * conv_w[w] for w in range(CONV_W))
    h = jax.nn.gelu(conv) * bv
    x = _ln(ALPHA * x + g2 * (h @ w_down), ln2_g, ln2_b)
    return x, (ka, va, logf, ret_new, a_ext[:, a_ext.shape[1] - (CONV_W - 1):])

def setup_inputs(seed: int = 0) -> dict:
    key = jax.random.key(seed)
    ks = jax.random.split(key, 32)
    f32 = jnp.float32
    n_pages = PAST_LEN // PAGE_SIZE
    n_used = DEC_BATCH * n_pages
    n_pool = n_used + max(1, n_used // 4)

    def nrm(k, shape, scale=1.0):
        return jax.random.normal(k, shape, f32) * scale

    x_prompt = nrm(ks[0], (BATCH, SEQ, D_MODEL))
    x_sample = nrm(ks[1], (DEC_BATCH, DEC_SEQ, D_MODEL))
    cache_k = nrm(ks[2], (DEPTH, n_pool, PAGE_SIZE, H_A, DH_A))
    cache_v = nrm(ks[3], (DEPTH, n_pool, PAGE_SIZE, H_A, DH_A))
    cache_logf = jax.nn.log_sigmoid(3.0 + nrm(ks[4], (DEPTH, n_pool, PAGE_SIZE, H_A)))
    state_ret = nrm(ks[5], (DEPTH, DEC_BATCH, H_R, DK_R, DV_R), 0.3)
    state_conv = nrm(ks[6], (DEPTH, DEC_BATCH, CONV_W - 1, D_FF))
    page_table = jax.random.permutation(ks[7], n_pool)[:n_used].reshape(DEC_BATCH, n_pages).astype(jnp.int32)
    c_prompt = nrm(ks[8], (BATCH, D_MODEL))
    c_sample = nrm(ks[9], (DEC_BATCH, D_MODEL))
    w_ada = nrm(ks[10], (DEPTH, D_MODEL, 6 * D_MODEL), 0.5 * D_MODEL ** -0.5)
    b_ada = nrm(ks[11], (DEPTH, 6 * D_MODEL), 0.02)
    w_in = nrm(ks[12], (DEPTH, D_MODEL, N_IN), D_MODEL ** -0.5)
    b_f = 3.0 + nrm(ks[13], (DEPTH, H_A), 0.1)
    w_pa = nrm(ks[14], (DEPTH, W_A, D_MODEL), W_A ** -0.5)
    w_pb = nrm(ks[15], (DEPTH, W_R, D_MODEL), W_R ** -0.5)
    w_o = nrm(ks[16], (DEPTH, D_MODEL, D_MODEL), BETA * D_MODEL ** -0.5)
    ln1_g = 1.0 + nrm(ks[17], (DEPTH, D_MODEL), 0.02)
    ln1_b = nrm(ks[18], (DEPTH, D_MODEL), 0.02)
    w_up = nrm(ks[19], (DEPTH, D_MODEL, 2 * D_FF), D_MODEL ** -0.5)
    conv_w = nrm(ks[20], (DEPTH, CONV_W, D_FF), CONV_W ** -0.5)
    conv_b = nrm(ks[21], (DEPTH, D_FF), 0.02)
    w_down = nrm(ks[22], (DEPTH, D_FF, D_MODEL), BETA * D_FF ** -0.5)
    ln2_g = 1.0 + nrm(ks[23], (DEPTH, D_MODEL), 0.02)
    ln2_b = nrm(ks[24], (DEPTH, D_MODEL), 0.02)
    return {'x_prompt': x_prompt, 'x_sample': x_sample, 'cache_k': cache_k, 'cache_v': cache_v,
            'cache_logf': cache_logf, 'state_ret': state_ret, 'state_conv': state_conv,
            'page_table': page_table, 'c_prompt': c_prompt, 'c_sample': c_sample,
            'w_ada': w_ada, 'b_ada': b_ada, 'w_in': w_in, 'b_f': b_f, 'w_pa': w_pa, 'w_pb': w_pb,
            'w_o': w_o, 'ln1_g': ln1_g, 'ln1_b': ln1_b, 'w_up': w_up, 'conv_w': conv_w,
            'conv_b': conv_b, 'w_down': w_down, 'ln2_g': ln2_g, 'ln2_b': ln2_b}

def reference(x_prompt, x_sample, cache_k, cache_v, cache_logf, state_ret, state_conv, page_table,
              c_prompt, c_sample, w_ada, b_ada, w_in, b_f, w_pa, w_pb, w_o, ln1_g, ln1_b,
              w_up, conv_w, conv_b, w_down, ln2_g, ln2_b):
    B = x_prompt.shape[0]
    Bs = x_sample.shape[0]
    P = page_table.shape[1] * cache_k.shape[2]
    hp, hs = x_prompt, x_sample
    kp_l, vp_l, lp_l, rp_l, cp_l = [], [], [], [], []
    ks_l, vs_l, ls_l, rs_l, cs_l = [], [], [], [], []
    for l in range(DEPTH):
        w = (w_ada[l], b_ada[l], w_in[l], b_f[l], w_pa[l], w_pb[l], w_o[l], ln1_g[l], ln1_b[l],
             w_up[l], conv_w[l], conv_b[l], w_down[l], ln2_g[l], ln2_b[l])
        ret0 = jnp.zeros((B, H_R, DK_R, DV_R), jnp.float32)
        conv0 = jnp.zeros((B, CONV_W - 1, D_FF), hp.dtype)
        hp, (k1, v1, lf1, r1, cv1) = _layer(hp, c_prompt, 0, None, ret0, conv0, *w)
        past = (cache_k[l][page_table].reshape(Bs, P, H_A, DH_A),
                cache_v[l][page_table].reshape(Bs, P, H_A, DH_A),
                cache_logf[l][page_table].reshape(Bs, P, H_A))
        hs, (k2, v2, lf2, r2, cv2) = _layer(hs, c_sample, P, past, state_ret[l], state_conv[l], *w)
        kp_l.append(k1); vp_l.append(v1); lp_l.append(lf1); rp_l.append(r1); cp_l.append(cv1)
        ks_l.append(k2); vs_l.append(v2); ls_l.append(lf2); rs_l.append(r2); cs_l.append(cv2)
    y_prompt, y_sample = hp, hs
    k_prompt, v_prompt, logf_prompt = jnp.stack(kp_l), jnp.stack(vp_l), jnp.stack(lp_l)
    ret_prompt, conv_prompt = jnp.stack(rp_l), jnp.stack(cp_l)
    k_sample, v_sample, logf_sample = jnp.stack(ks_l), jnp.stack(vs_l), jnp.stack(ls_l)
    ret_sample, conv_sample = jnp.stack(rs_l), jnp.stack(cs_l)
    return (y_prompt, y_sample, k_prompt, v_prompt, logf_prompt, ret_prompt, conv_prompt,
            k_sample, v_sample, logf_sample, ret_sample, conv_sample)


_drawn_inputs = setup_inputs


def setup_inputs(seed=0):
    import zlib

    import numpy as np

    out = dict(_drawn_inputs(seed))
    spreads = {}
    factors = {'cache_k': 3.943,
     'cache_v': 3.141,
     'cache_logf': 8.0,
     'ln1_g': 7.571,
     'ln1_b': 7.599,
     'conv_b': 26.196,
     'ln2_g': 8.239,
     'ln2_b': 8.147}
    for name, (base, spread) in spreads.items():
        noise = np.random.default_rng([zlib.crc32(name.encode()), seed]).standard_normal(out[name].shape)
        drawn = base * np.exp(spread * noise) if base else spread * noise
        out[name] = __import__('jax').numpy.asarray(drawn.astype(out[name].dtype))
    for name, factor in factors.items():
        out[name] = (out[name] * factor).astype(out[name].dtype)
    return out
```

```python
from contextlib import ExitStack

import numpy as np

import concourse.bass as bass
from concourse import mybir

ALU = mybir.AluOpType
ACT = mybir.ActivationFunctionType
AX_X = mybir.AxisListType.X
F32 = mybir.dt.float32
F32R = mybir.dt.float32r

P = 128
D = 2048
KD = D // P
TP = 256
NB, TS = 8, 8
NS = NB * TS
T = TP + NS
H = 8
DH = 128
PAGE = 128
NPG = 2
DFF = 5632
KF = DFF // P
HALF = KF // 2
NSEQ = 1 + NB
ALPHA = 2.0 ** 0.25
EPS = 1e-5
MASKED = -1e30

CB = 8
CW = CB * P
RING = 4
CROW = 10
N_GROUP = 4
UNITS = ["qr", "ada", "kr", "ada", "vr", "ada", "gr", "ada", "qa", "ada", "ka", "ada", "va", "ada", "ada"]
GEMMS = [u for u in UNITS if u != "ada"]
PRE = 4
N_ADA = 2 * 2 * KD
N_HEAD = 2 * len(UNITS)
ADA0 = 0
HEADS0 = ADA0 + N_ADA
GATES0 = HEADS0 + H * N_HEAD
BRANCH0 = GATES0 + 4 * PRE
MERGE0 = BRANCH0 + 2 * PRE
OUT0 = MERGE0 + 6 * (KD - PRE)
UP0 = OUT0 + 2 * KD
N_UP, N_DOWN = 4 * HALF, 3 * KD
DOWN0 = UP0 + N_UP
UP1 = DOWN0 + N_DOWN
DOWN1 = UP1 + N_UP
CHUNKS = DOWN1 + N_DOWN
DOWN_BLOCKS = [8, 8, HALF - 16]

JOBS = ["v_rows", "kr_rows", "vr_rows", "scores", "past_scores", "ret_scores", "row_scores", "ret_state",
        "probs_t", "ret_out", "row_probs_t", "center", "variance", "state0", "state1", "attend"]
JOB = {name: k for k, name in enumerate(JOBS)}
STEP_PE = {0: ["v_rows", "kr_rows"], 1: ["vr_rows"], 2: ["scores", "past_scores"], 3: ["ret_scores"],
           4: ["row_scores"], 5: ["ret_state"], 6: ["probs_t", "ret_out"], 7: ["row_probs_t"], 8: ["center"],
           10: ["variance"], 11: ["state0"], 12: ["state1", "attend"]}
STEP_ACT = {0: ["v_rows"], 1: ["vr_rows"], 2: ["past_scores"], 3: ["exp"], 5: ["row_exp", "ret_state"],
            6: ["probs_t", "ret_out"], 7: ["row_probs_t"], 8: ["center"], 10: ["variance"], 12: ["attend"],
            14: ["ob_hi"]}
STEP_DVE = {0: ["gather", "kr_rows"], 2: ["scores"], 3: ["ret_scores"], 4: ["row_scores", "normalise"],
            6: ["row_normalise"], 8: ["center"], 10: ["deviation"], 11: ["state0"], 12: ["state1", "attend"],
            14: ["ob_lo"]}
STAGE_AT = {3: 0, 7: 1, 11: 2, 14: 3}
TURN_AT = {4: 0, 8: 1, 12: 2, 0: 3}
BIAS_AT = {5: 0, 9: 1, 13: 2, 1: 3}
LAST_PE = {0: ["v_rows", "kr_rows", "vr_rows"], 1: ["scores", "past_scores", "ret_scores"],
           2: ["row_scores", "ret_state"], 3: ["probs_t", "ret_out"],
           4: ["row_probs_t", "center"], 5: ["variance", "state0", "state1"], 6: ["attend"]}
LAST_ACT = {0: ["v_rows", "vr_rows"], 1: ["past_scores"], 2: ["exp", "row_exp", "ret_state"],
            3: ["probs_t", "ret_out"], 4: ["row_probs_t", "center"], 5: ["variance"], 6: ["attend"], 7: ["ob_hi"]}
LAST_DVE = {0: ["gather", "kr_rows"], 1: ["scores", "ret_scores"], 2: ["row_scores", "normalise"],
            3: ["row_normalise"], 4: ["center"], 5: ["deviation", "state0", "state1"], 6: ["attend"],
            7: ["ob_lo"]}

C_IDENT, C_CENTER, C_MEAN, C_AFTER = 0, 128, 256, 384
C_NEGTRI = 512
C_MASK = 768
C_ROWMASK = 1024
C_NEGTRI_SEQ = 1344
C_SEQ = 1408
C_EPS, C_ONE = 1416, 1417
C_SUM = 1418
N_CONST = 1428
T_SEQ, T_CROSS, T_KW, T_DECAY = 256, 320, 384, 387
N_TAB = 388


def at(base, i=None, period=0):
    return base if i is None else base + i * period


def build(nc, a):
    sb_base = 16512
    top = [sb_base]
    limit = nc.sbuf_usable_end

    def place(name, shape, dt=F32, offset=None):
        size = int(np.prod(shape[1:])) * 4
        if offset is None:
            offset = top[0]
            top[0] += -(-size // 32) * 32
        assert offset + size <= limit, (name, offset, size, limit)
        return nc.alloc_sbuf_tensor_at(name, shape, dt, offset=offset)

    raw = [place(f"raw{s}", [P, CB, P]) for s in range(RING)]
    w_hi = [place(f"w_hi{s}", [P, CB, P], F32R) for s in range(RING)]
    w_lo = [place(f"w_lo{s}", [P, CB, P], F32R) for s in range(RING)]
    u_hi = place("u_hi", [P, KD, T], F32R)
    u_lo = place("u_lo", [P, KD, T], F32R)
    region_x = top[0]
    top[0] += 2 * KD * T * 4
    consts = place("consts", [P, N_CONST])
    mod = place("mod", [P, 6 * KD, NSEQ])
    b_ada = place("b_ada", [P, 6 * KD])
    ln = place("ln", [P, 4, KD])
    region_h = top[0]

    x = place("x", [P, KD, T], offset=region_x)
    half_x = region_x + KD * T * 4
    c_raw = place("c_raw", [P, KD, NSEQ], offset=half_x)
    c_exp = place("c_exp", [P, KD, NSEQ], offset=half_x + 640)
    w_f = place("w_f", [P, KD, H], offset=half_x + 1280)
    b_f = place("b_f", [P, H], offset=half_x + 1792)
    f_z = place("f_z", [P, 3, H], offset=half_x + 1824)
    f_t = place("f_t", [P, 3, H], offset=half_x + 1920)
    oa_hi = place("oa_hi", [P, H, T], F32R, offset=region_x)
    oa_lo = place("oa_lo", [P, H, T], F32R, offset=region_x + H * T * 4)
    ob_hi = place("ob_hi", [P, H, T], F32R, offset=half_x)
    ob_lo = place("ob_lo", [P, H, T], F32R, offset=half_x + H * T * 4)
    r = place("r", [P, KD, T], offset=region_x)

    def scratch(base):
        cur = [base]

        def take(name, shape, dt=F32):
            o = cur[0]
            cur[0] += -(-int(np.prod(shape[1:])) * 4 // 32) * 32
            return place(name, shape, dt, offset=o)
        return take, cur

    take, _ = scratch(half_x)
    EXT = 2 + TP + NB * (2 + TS)
    a_ext = [take(f"a_ext{q}", [P, EXT]) for q in range(2)]
    conv = [take(f"conv{q}", [P, EXT]) for q in range(2)]
    h_f = take("h_f", [P, T])
    ln_sum = take("ln_sum", [P, T])
    ln_mean = take("ln_mean", [P, T])
    ln_var = take("ln_var", [P, T])
    ln_sq = [take(f"ln_sq{q}", [P, 2, T]) for q in range(2)]
    u2_f = [take(f"u2_f{q}", [P, T]) for q in range(2)]
    y_t = take("y_t", [P, T])

    take, cur = scratch(region_h)
    kv = take("kv", [P, NB * NPG, 2 * P])
    state = take("state", [P, NB, DH])
    tab = [take(f"tab{q}", [P, N_TAB]) for q in range(2)]
    v_rows = take("v_rows", [P, 3, DH])
    kr_rows = take("kr_rows", [P, 3, DH])
    vr_rows = take("vr_rows", [P, 3, DH])
    v_seq = take("v_seq", [NS, NB, DH])
    probs = take("probs", [P, 384])
    probs_t = take("probs_t", [P, 384])
    past_t = probs_t[:, 0:P]
    att = take("att", [P, 448])
    row_p = take("row_p", [NS, T])
    row_pt = take("row_pt", [P, 192])
    o_ret = take("o_ret", [P, T])
    o_cen = take("o_cen", [P, T])
    o_sq = att[:, 0:T]
    o_var = take("o_var", [P, T])
    q_dec = take("q_dec", [P, NS])
    swap = take("swap", [P, T])
    g_exp = take("g_exp", [P, T])
    state_p = take("state_p", [P, DH])
    lf_h = take("lf_h", [P, 3])
    lfp_h = take("lfp_h", [P, NB * NPG])
    smx = take("smx", [P, 4])
    srow = take("srow", [P, 4])
    ssum = take("ssum", [P, 4])
    lf = take("lf", [P, 3, H])
    lfp = take("lfp", [P, NB * NPG, H])
    c_hl = take("c_hl", [P, (KD - 1) * 2 * CROW + P], F32R)
    c_parts = c_hl[:, 0:KD * 2 * CROW].rearrange("p (k c) -> p k c", c=2 * CROW)
    ada_rows = take("ada_rows", [2 * CROW, 2 * P])
    cossin = take("cossin", [P, 2, T])
    qkv_at = cur[0] = max(cur[0], region_h + 3 * KD * T * 4 - 7 * T * 4)
    tiles = [{u: take(f"{u}{q}", [P, T]) for u in GEMMS} for q in (1, 0)][::-1]
    gate_at = qkv_at + 7 * T * 4
    gate = [place(f"gate{n}", [P, T], offset=gate_at + n * T * 4) for n in range(2 * PRE)]
    assert region_h + 3 * KD * T * 4 <= gate_at, (gate_at - region_h, 3 * KD * T * 4)
    m_hi = place("m_hi", [P, KD, T], F32R, offset=region_h)
    m_lo = place("m_lo", [P, KD, T], F32R, offset=region_h + KD * T * 4)
    x_again = place("x_again", [P, KD, T], offset=region_h + 2 * KD * T * 4)
    take, _ = scratch(region_h)
    h_hi = take("h_hi", [P, HALF, T], F32R)
    h_lo = take("h_lo", [P, HALF, T], F32R)
    w_conv = take("w_conv", [P, KF, 4])
    s_conv = take("s_conv", [P, KF, NB, 2])
    conv_out = take("conv_out", [P, KF, NSEQ, 2])
    ln_a = take("ln_a", [P, KD, NSEQ])
    ln_c = take("ln_c", [P, KD, NSEQ])

    def c_(col, n, rows=P):
        return consts[0:rows, col:col + n]

    ctx = ExitStack()
    with ctx:
        banks = [ctx.enter_context(nc.psum_tensor(f"bank{b}", [P, 512], F32)) for b in range(8)]
        ADA_BANK, LOGF_BANK, MOD_BANK = banks[2], banks[7], banks[7]
        WORK = banks[3:7]

        def sem(name):
            return ctx.enter_context(nc.semaphore(name))

        landed = [sem(f"landed{s}") for s in range(RING)]
        hi_made, lo_made, used = sem("hi_made"), sem("lo_made"), sem("used")
        x_in, c_in, small_in, pages_in = sem("x_in"), sem("c_in"), sem("small_in"), sem("pages_in")
        x_again_in, ffn_in = sem("x_again_in"), sem("ffn_in")
        c_exp_made, c_silu, c_hi_made, c_ready = sem("c_exp_made"), sem("c_silu"), sem("c_hi_made"), sem("c_ready")
        bias_one, ada_staged, ada_turned = sem("bias_one"), sem("ada_staged"), sem("ada_turned")
        mod_made = sem("mod_made")
        u_prompt, u_mul, u_f32 = sem("u_prompt"), sem("u_mul"), sem("u_f32")
        u_hi_made, u_lo_made = sem("u_hi_made"), sem("u_lo_made")
        f_done, f_zero, f_z_made, f_abs, f_exp = sem("f_done"), sem("f_zero"), sem("f_z_made"), sem("f_abs"), sem("f_exp")
        f_one, f_ln, lf_ready, lf_out = sem("f_one"), sem("f_ln"), sem("lf_ready"), sem("lf_out")
        plain = sem("plain")
        swapped, rope_step, roped = sem("swapped"), sem("rope_step"), sem("roped")
        g_exp_made, g_one, g_inv, g_silu = sem("g_exp_made"), sem("g_one"), sem("g_inv"), sem("g_silu")
        kv_out = [sem("kv_out0"), sem("kv_out1")]
        k_in, v_in, state_in = sem("k_in"), sem("v_in"), sem("state_in")
        tab_in = [sem("tab_in0"), sem("tab_in1")]
        state_out, state_p_out = sem("state_out"), sem("state_p_out")
        written = [sem(f"written{w}") for w in range(4)]
        taken = [sem(f"taken{w}") for w in range(4)]
        gathered, neg_made, exp_made = sem("gathered"), sem("neg_made"), sem("exp_made")
        inv_made, probs_made = sem("inv_made"), sem("probs_made")
        row_neg_made, row_exp_made = sem("row_neg_made"), sem("row_exp_made")
        row_inv_made, row_probs_made = sem("row_inv_made"), sem("row_probs_made")
        v_seq_made = sem("v_seq_made")
        oa_hi_made = sem("oa_hi_made")
        sq_made, o_rstd, ob_step, ob_f32 = sem("sq_made"), sem("o_rstd"), sem("ob_step"), sem("ob_f32")
        ob_hi_made, ob_made = sem("ob_hi_made"), sem("ob_made")
        gate_exp, gate_one, gate_made = sem("gate_exp"), sem("gate_one"), sem("gate_made")
        branch_read, sum_made = sem("branch_read"), sem("sum_made")
        m_hi_made, m_made = sem("m_hi_made"), sem("m_made")
        proj_read, scaled, r_made, summed = sem("proj_read"), sem("scaled"), sem("r_made"), sem("summed")
        mean_done, mean_made, centered = sem("mean_done"), sem("mean_made"), sem("centered")
        squared, sq_used, deviation = sem("squared"), sem("sq_used"), sem("deviation")
        rstd_made, normed, ln_factors = sem("rstd_made"), sem("normed"), sem("ln_factors")
        u2_prompt, u2_mul, u2_sample = sem("u2_prompt"), sem("u2_mul"), sem("u2_sample")
        u2_hi_made, u2_made, x1_made = sem("u2_hi_made"), sem("u2_made"), sem("x1_made")
        ext_zero, a_read, hist, kept = sem("ext_zero"), sem("a_read"), sem("hist"), sem("kept")
        conv_step, conv_made, gelu_made = sem("conv_step"), sem("conv_made"), sem("gelu_made")
        hf_made, h_hi_made, h_made = sem("hf_made"), sem("h_hi_made"), sem("h_made")
        y_made, y_out = sem("y_made"), sem("y_out")
        passed = {}

        block = ctx.enter_context(nc.Block())

        def seqs(ap):
            return ap.rearrange("p (b t) -> p b t", b=NB)

        def per_seq(ap):
            return ap.unsqueeze(2).to_broadcast([ap.shape[0], NB, TS])

        def rep(ap, n):
            return ap.unsqueeze(1).to_broadcast([ap.shape[0], n, ap.shape[1]])

        def histories(e):
            return e[:, 2 + TP:EXT].rearrange("p (b t) -> p b t", b=NB)

        def settle(eng):
            if eng not in passed:
                passed[eng] = sem(f"passed{len(passed)}")
            eng.sem_inc(passed[eng], 1)

        def is_written(eng, job, h):
            k = JOB[job]
            eng.wait_ge(written[k % 4], 4 * h + (k // 4 + 1))

        def is_taken(eng, job, h):
            k = JOB[job]
            eng.wait_ge(taken[k % 4], 4 * h + (k // 4 + 2))

        def tile_is_read(eng, name, h):
            if name in ("qr", "kr"):
                eng.wait_ge(swapped, 2 * h + (1 if name == "qr" else 2))
            elif name == "gr":
                eng.wait_ge(g_exp_made, h + 1)
            else:
                eng.wait_ge(plain, 4 * h + ("vr", "qa", "ka", "va").index(name) + 1)

        def chunk_used(eng, n):
            eng.wait_ge(used, n + 1)

        @block.sync
        def _(sp):
            def load(base, i=None, period=0, blocks=CB):
                n = at(base, i, period)
                if i is not None or n >= RING:
                    sp.wait_ge(lo_made, n - (RING - 1))
                sp.dma_start(raw[base % RING][:, 0:blocks, :],
                             a["w"][n, :, 0:blocks * P].rearrange("p (k c) -> p k c", k=blocks)
                             ).then_inc(landed[base % RING], 16)

            def stream(first, end, blocks=(CB,)):
                body = RING * len(blocks)
                with sp.Fori(0, (end - first) // body) as i:
                    for n in range(body):
                        load(first + n, i, body, blocks[n % len(blocks)])

            sp.dma_start(c_raw[:], a["c"]).then_inc(c_in, 16)
            sp.dma_start(b_ada[:], a["b_ada"]).then_inc(c_in, 16)
            for n in range(RING):
                load(n)
            sp.dma_start(x[:], a["x"]).then_inc(x_in, 16)
            for dst, src in ((consts[:], a["consts"]), (cossin[:], a["cossin"]), (w_f[:], a["w_f"]),
                             (b_f[:], a["b_f"].partition_broadcast(P)), (ln[:], a["ln"])):
                sp.dma_start(dst, src).then_inc(small_in, 16)
            page = [sp.value_load(a["pages"][0:1, n:n + 1], min_val=0, max_val=a["cache_lf"].shape[0] - 1)
                    for n in range(NB * NPG)]
            for n in range(NB * NPG):
                sp.dma_start(lfp[:, n, :], a["cache_lf"][page[n], :, :]).then_inc(pages_in, 16)
            stream(RING, HEADS0)

            def pages_of(h, half, count):
                for n in range(NB * NPG):
                    sp.dma_start(kv[:, n, half * P:(half + 1) * P],
                                 a["cache_kv"][page[n], h, half, :, :]).then_inc(count, 16)

            def for_next_step(u, h, q):
                if u == 6:
                    if not isinstance(h, int) or h >= 2:
                        is_taken(sp, "state1", h - 2)
                    sp.dma_start(tab[q][:], a["tab"][h, :, :]).then_inc(tab_in[q], 16)
                if u == 8:
                    if not isinstance(h, int) or h >= 1:
                        is_taken(sp, "past_scores", h - 1)
                    pages_of(h, 0, k_in)

            def for_attention(u, h, first):
                if u == 2:
                    if not first:
                        sp.wait_ge(state_out, h * 16)
                    sp.dma_start(state[:], a["state"][:, h, :, :].rearrange("b d e -> d b e")).then_inc(state_in, 16)
                if u == 3:
                    if not first:
                        sp.wait_ge(oa_hi_made, h)
                    pages_of(h, 1, v_in)

            def step(base, i, period, h, q, attention, first=False):
                for u in range(len(UNITS)):
                    for c in range(2):
                        load(base + 2 * u + c, i, period)
                    for_next_step(u, h, q)
                    if attention:
                        for_attention(u, h - 1, first)

            step(HEADS0, None, 0, 0, 0, False)
            step(HEADS0 + N_HEAD, None, 0, 1, 1, True, True)
            with sp.Fori(0, 3) as i:
                step(HEADS0 + 2 * N_HEAD, i, 2 * N_HEAD, i * 2 + 2, 0, True)
                step(HEADS0 + 3 * N_HEAD, i, 2 * N_HEAD, i * 2 + 3, 1, True)
            for n in range(GATES0, MERGE0):
                load(n)
                if n == GATES0 + 2:
                    for_attention(2, H - 1, False)
                if n == GATES0 + 3:
                    for_attention(3, H - 1, False)
            for n in range(MERGE0, MERGE0 + 12):
                load(n)
            sp.wait_ge(ob_made, H)
            is_taken(sp, "attend", H - 1)
            sp.wait_ge(state_p_out, 16 * H)
            sp.wait_ge(state_out, 16 * H)
            for q in range(2):
                sp.wait_ge(kv_out[q], 32 * (H // 2))
            sp.wait_ge(lf_out, 32)
            sp.dma_start(x_again[:], a["x"]).then_inc(x_again_in, 16)
            stream(MERGE0 + 12, OUT0)
            stream(OUT0, UP0)
            for n in range(UP0, UP0 + RING):
                load(n)
            sp.wait_ge(r_made, KD)
            sp.dma_start(w_conv[:], a["w_conv"]).then_inc(ffn_in, 16)
            sp.dma_start(s_conv[:], a["s_conv"]).then_inc(ffn_in, 16)
            stream(UP0 + RING, DOWN0)
            stream(DOWN0, UP1, DOWN_BLOCKS)
            stream(UP1, DOWN1)
            stream(DOWN1, CHUNKS, DOWN_BLOCKS)
            for g in range(4):
                sp.wait_ge(y_made, 4 * g + 4)
                sp.dma_start(a["y"][:, 4 * g:4 * g + 4, :], r[:, 4 * g:4 * g + 4, :]).then_inc(y_out, 16)
            sp.wait_ge(kept, 4 + 2 * KF)
            sp.dma_start(a["conv"], conv_out[:]).then_inc(y_out, 16)
            sp.wait_ge(y_out, 5 * 16)

        @block.gpsimd
        def _(pool):
            for w in range(4):
                pool.sem_inc(taken[w], 1)
            pool.sem_inc(ada_staged, 1)
            pool.sem_inc(ada_turned, 1)
            pool.sem_inc(mod_made, 2)
            pool.sem_inc(proj_read, 2)
            pool.sem_inc(a_read, 4)
            pool.sem_inc(hf_made, 4)
            pool.sem_inc(conv_made, 2)
            pool.sem_inc(kept, 4)
            nc.gpsimd.memset(c_hl[:].bitcast(F32), 0.0).then_inc(c_ready, 1)
            pool.wait_ge(x_in, 16)
            with pool.Fori(0, KD // 2) as g:
                pool.wait_ge(mod_made, g * 4 + 6)
                for q in range(2):
                    k = g * 2 + q
                    xs = seqs(x[:, k, TP:T])
                    nc.gpsimd.tensor_tensor(xs, xs, per_seq(mod[:, k + KD, 1:NSEQ]), ALU.mult).then_inc(u_mul, 1)
                    pool.wait_ge(u_mul, k + 1)
                    nc.gpsimd.tensor_tensor(xs, xs, per_seq(mod[:, k, 1:NSEQ]), ALU.add).then_inc(u_f32, 1)
                for q in range(2):
                    k = g * 2 + q
                    pool.wait_ge(u_hi_made, k + 1)
                    nc.gpsimd.tensor_tensor(u_lo[:, k, :], x[:, k, :], u_hi[:, k, :].bitcast(F32),
                                            ALU.subtract).then_inc(u_lo_made, 1)

            def rope(name, q, n):
                t = tiles[q][name]
                pool.wait_ge(swapped, n + 1)
                nc.gpsimd.tensor_tensor(t[:], t[:], cossin[:, 0, :], ALU.mult).then_inc(rope_step, 1)
                nc.gpsimd.tensor_tensor(swap[:], swap[:], cossin[:, 1, :], ALU.mult).then_inc(rope_step, 1)
                pool.wait_ge(rope_step, n * 2 + 2)
                nc.gpsimd.tensor_tensor(t[:], t[:], swap[:], ALU.add).then_inc(roped, 1)

            def products(u, h, q):
                if UNITS[u] in ("qr", "kr"):
                    rope(UNITS[u], q, 2 * h + (UNITS[u] == "kr"))
                if u == 7:
                    pool.wait_ge(g_inv, h + 1)
                    t = tiles[q]["gr"]
                    nc.gpsimd.tensor_tensor(t[:], t[:], g_exp[:], ALU.mult).then_inc(g_silu, 1)
                if u == 14:
                    pool.wait_ge(plain, 4 * h + 4)
                    settle(pool)
                    for n, name in enumerate(("ka", "va")):
                        pool.dma_start(a["kv_new"][n, h, :, :], tiles[q][name][:]).then_inc(kv_out[q], 16)

            def attention(u, h, q):
                if u == 1:
                    is_taken(pool, "vr_rows", h)
                    nc.gpsimd.tensor_tensor(v_seq[:], rep(vr_rows[0:NS, 2, :], NB),
                                            c_(C_SEQ, NB, NS).unsqueeze(2).to_broadcast([NS, NB, DH]),
                                            ALU.mult).then_inc(v_seq_made, 1)
                if u == 5:
                    is_taken(pool, "ret_state", h)
                    settle(pool)
                    pool.dma_start(a["ret_prompt"][h, :, :], state_p[:]).then_inc(state_p_out, 16)
                if u == 12:
                    is_taken(pool, "state1", h)
                    settle(pool)
                    pool.dma_start(a["ret_sample"][:, h, :, :].rearrange("b d e -> d b e"),
                                   state[:]).then_inc(state_out, 16)
                if u == 11:
                    pool.wait_ge(g_silu, h + 1)
                    is_taken(pool, "center", h)
                    nc.gpsimd.tensor_tensor(o_cen[:], o_cen[:], tiles[q]["gr"][:], ALU.mult).then_inc(ob_step, 1)
                    pool.wait_ge(ob_step, h + 1)
                    pool.wait_ge(o_rstd, h + 1)
                    nc.gpsimd.tensor_tensor(o_cen[:], o_cen[:], o_var[:], ALU.mult).then_inc(ob_f32, 1)

            def step(h, q, has_products, has_attention):
                for u in range(len(UNITS)):
                    if has_products:
                        products(u, h, q)
                    if has_attention:
                        attention(u, h - 1, 1 - q)

            pool.wait_ge(small_in, 80)
            step(0, 0, True, False)
            pool.wait_ge(lf_ready, 1)
            pool.dma_start(a["lf_prompt"].rearrange("(c p) h -> p c h", p=P), lf[:, 0:2, :]).then_inc(lf_out, 16)
            pool.dma_start(a["lf_sample"], lf[0:NS, 2, :]).then_inc(lf_out, 16)
            step(1, 1, True, True)
            with pool.Fori(0, 3) as i:
                step(i * 2 + 2, 0, True, True)
                step(i * 2 + 3, 1, True, True)
            step(8, 0, False, True)

            chunk_used(pool, OUT0 - 1)
            nc.gpsimd.memset(ln_sum[:], 0.0).then_inc(summed, 1)
            with pool.Fori(0, KD) as k:
                pool.wait_ge(r_made, k + 1)
                pool.wait_ge(summed, k + 1)
                nc.gpsimd.tensor_tensor(ln_sum[:], ln_sum[:], r[:, k, :], ALU.add).then_inc(summed, 1)
            pool.wait_ge(mod_made, 6 * KD + 2)
            scale2 = mod[:, 4 * KD:5 * KD, :]
            for dst, w in ((ln_a, 0), (ln_c, 1)):
                nc.gpsimd.tensor_tensor(dst[:], scale2, ln[:, w, :].unsqueeze(2).to_broadcast([P, KD, NSEQ]),
                                        ALU.mult).then_inc(ln_factors, 1)
            pool.wait_ge(ln_factors, 2)
            nc.gpsimd.tensor_tensor(ln_c[:], ln_c[:], mod[:, 3 * KD:4 * KD, :], ALU.add).then_inc(ln_factors, 1)
            for q in range(2):
                nc.gpsimd.memset(a_ext[q][:], 0.0).then_inc(ext_zero, 1)
            pool.wait_ge(ln_factors, 3)
            for k in range(KD):
                pool.wait_ge(normed, k // 2 + 1)
                if k >= 2:
                    pool.wait_ge(u2_made, k - 1)
                us = seqs(u2_f[k % 2][:, TP:T])
                nc.gpsimd.tensor_tensor(us, seqs(r[:, k, TP:T]), per_seq(ln_a[:, k, 1:NSEQ]),
                                        ALU.mult).then_inc(u2_mul, 1)
                pool.wait_ge(u2_mul, k + 1)
                nc.gpsimd.tensor_tensor(us, us, per_seq(ln_c[:, k, 1:NSEQ]), ALU.add).then_inc(u2_sample, 1)
            nc.gpsimd.memset(ln_sum[:], 0.0).then_inc(summed, 1)
            pool.wait_ge(ext_zero, 2)
            pool.wait_ge(ffn_in, 32)

            with pool.Fori(0, KF // 2) as i:
                for q in range(2):
                    n = i * 2 + q
                    pool.wait_ge(conv_made, n + 1)
                    pool.wait_ge(kept, n * 2 + 2)
                    nc.gpsimd.tensor_copy(histories(a_ext[q])[:, :, 0:2], s_conv[:, n, :, :]).then_inc(hist, 1)
                    pool.wait_ge(a_read, n * 2 + 6)
                    nc.gpsimd.tensor_copy(conv_out[:, n, 0, :], a_ext[q][:, TP:TP + 2]).then_inc(kept, 1)
                    nc.gpsimd.tensor_copy(conv_out[:, n, 1:NSEQ, :],
                                          histories(a_ext[q])[:, :, TS:TS + 2]).then_inc(kept, 1)
            with pool.Fori(0, KD) as k:
                pool.wait_ge(r_made, k + (2 * KD + 1))
                pool.wait_ge(summed, k + (KD + 2))
                nc.gpsimd.tensor_tensor(ln_sum[:], ln_sum[:], r[:, k, :], ALU.add).then_inc(summed, 1)

        @block.scalar
        def _(act):
            def split(base, i=None, period=0):
                if base >= CHUNKS:
                    return
                n, s = at(base, i, period), base % RING
                if i is not None or n >= RING:
                    act.wait_ge(used, n - (RING - 1))
                act.wait_ge(landed[s], at(16 * (base // RING + 1), i, 16 * (period // RING)))
                nc.scalar.activation(w_hi[s][:], raw[s][:], ACT.Copy).then_inc(hi_made, 1)

            def copy(out, in_, scale=1.0):
                return nc.scalar.activation(out, in_, ACT.Copy, scale=scale)

            act.wait_ge(c_in, 32)
            nc.scalar.activation(c_exp[:], c_raw[:], ACT.Exp, scale=-1.0).then_inc(c_exp_made, 1)
            for n in range(2):
                split(n)
            act.wait_ge(c_silu, 3)
            act.wait_ge(c_ready, 1)
            copy(c_parts[:, :, 0:NSEQ], c_raw[:]).then_inc(c_hi_made, 1)
            for n in range(2, RING):
                split(n)

            def add_bias(group, m):
                act.wait_ge(ada_turned, group + 2)
                for j in range(2):
                    nc.scalar.activation(mod[:, bass.ds(m + j, 1), :], MOD_BANK[:, CROW * j:CROW * j + NSEQ],
                                         ACT.Identity, bias=b_ada[:, bass.ds(m + j, 1)]).then_inc(mod_made, 1)

            def make_u_hi(g):
                for q in range(2):
                    k = g * 2 + q
                    act.wait_ge(u_prompt, k + 1)
                    act.wait_ge(u_f32, k + 1)
                    copy(u_hi[:, k, :], x[:, k, :]).then_inc(u_hi_made, 1)

            def conditioning(base, i, g, first):
                for half in range(2):
                    split(base + RING + 4 * half, i, 8)
                    split(base + RING + 4 * half + 1, i, 8)
                    if half == 1:
                        add_bias(g * 2, g * 2)
                        if not first:
                            make_u_hi(g - 1)
                    elif not first:
                        add_bias(g * 2 - 1, g * 2 + (KD - 2))
                    split(base + RING + 4 * half + 2, i, 8)
                    split(base + RING + 4 * half + 3, i, 8)

            act.wait_ge(bias_one, 2)
            conditioning(ADA0, None, 0, True)
            with act.Fori(0, KD // 2 - 1) as i:
                conditioning(ADA0 + 8, i, i + 1, False)
            add_bias(KD - 1, 2 * KD - 2)
            make_u_hi(KD // 2 - 1)

            def products(u, base, i, period, h, q):
                name = UNITS[u]
                if u in BIAS_AT:
                    j = BIAS_AT[u] - 4 * (u == 1)
                    if not (isinstance(h, int) and 4 * h + j < 0):
                        add_bias(h * 4 + (KD + j), h * 8 + (2 * KD + 2 * j))
                if name == "ada":
                    return
                g = GEMMS.index(name)
                t = tiles[q][name]
                bank = banks[(q + g) % 2]
                chunk_used(act, at(base + 1, i, period))
                if name in ("qr", "kr"):
                    scale = DH ** -0.5 if name == "kr" else 1.0
                    turned = 2 * h + (name == "kr")
                    if not (isinstance(turned, int) and turned == 0):
                        act.wait_ge(roped, turned)
                    copy(t[:], bank[:, 0:T], scale)
                    copy(swap[0:64, :], bank[64:P, 0:T], scale)
                    copy(swap[64:P, :], bank[0:64, 0:T], scale).then_inc(swapped, 1)
                elif name == "gr":
                    if not (isinstance(h, int) and h == 0):
                        act.wait_ge(g_silu, h)
                    copy(t[:], bank[:, 0:T])
                    nc.scalar.activation(g_exp[:], bank[:, 0:T], ACT.Exp, scale=-1.0).then_inc(g_exp_made, 1)
                else:
                    if name in ("ka", "va") and not (isinstance(h, int) and h < 2):
                        act.wait_ge(kv_out[q], (h - q) * 16)
                    copy(t[:], bank[:, 0:T], DH ** -0.5 if name == "qa" else 1.0).then_inc(plain, 1)

            def attention(job, h, q):
                work = WORK[JOB[job] % 4] if job in JOB else None
                done = taken[JOB[job] % 4] if job in JOB else None
                if job in JOB:
                    is_written(act, job, h)
                if job == "v_rows":
                    copy(v_rows[:, 0:2, :], work[:, 0:256].rearrange("p (c d) -> p c d", c=2))
                    copy(v_rows[0:NS, 2, :], work[0:NS, 256:384]).then_inc(done, 1)
                elif job == "vr_rows":
                    copy(vr_rows[:, 0:2, :], work[:, 0:256].rearrange("p (c d) -> p c d", c=2))
                    copy(vr_rows[0:NS, 2, :], work[0:NS, 256:384]).then_inc(done, 1)
                elif job == "past_scores":
                    copy(past_t[:], work[:, 0:P]).then_inc(done, 1)
                elif job == "exp":
                    act.wait_ge(neg_made, h + 1)
                    nc.scalar.activation(probs[:, 0:128], probs[:, 0:128], ACT.Exp, bias=smx[:, 2:3],
                                         accum_out=ssum[:, 0:1])
                    nc.scalar.activation(probs[:, 128:384], probs[:, 128:384], ACT.Exp, bias=smx[:, 3:4],
                                         accum_out=ssum[:, 1:2]).then_inc(exp_made, 1)
                elif job == "row_exp":
                    act.wait_ge(row_neg_made, h + 1)
                    nc.scalar.activation(row_p[:], row_p[:], ACT.Exp, bias=srow[0:NS, 1:2],
                                         accum_out=srow[0:NS, 2:3]).then_inc(row_exp_made, 1)
                elif job == "ret_state":
                    if not (isinstance(h, int) and h == 0):
                        act.wait_ge(state_p_out, h * 16)
                    copy(state_p[:], work[:, 0:DH]).then_inc(done, 1)
                elif job == "probs_t":
                    copy(probs_t[:], work[:, 0:384]).then_inc(done, 1)
                elif job == "ret_out":
                    copy(o_ret[:], work[:, 0:T]).then_inc(done, 1)
                elif job == "row_probs_t":
                    copy(row_pt[:, 0:128], work[:, 0:128])
                    copy(row_pt[0:NS, 128:192], work[0:NS, 128:192]).then_inc(done, 1)
                elif job == "attend":
                    copy(oa_hi[:, h, :], work[:, 0:T]).then_inc(oa_hi_made, 1)
                elif job == "center":
                    nc.scalar.activation(o_sq, work[:, 0:T], ACT.Square).then_inc(sq_made, 1)
                elif job == "variance":
                    nc.scalar.activation(o_var[:], work[:, 0:T], ACT.Sqrt, bias=c_(C_EPS, 1)).then_inc(done, 1)
                elif job == "ob_hi":
                    act.wait_ge(ob_f32, h + 1)
                    copy(ob_hi[:, h, :], o_cen[:]).then_inc(ob_hi_made, 1)

            def forget_logits():
                act.wait_ge(f_abs, 1)
                nc.scalar.activation(f_t[:], f_t[:], ACT.Exp, scale=-1.0).then_inc(f_exp, 1)
                act.wait_ge(f_one, 1)
                nc.scalar.activation(f_t[:], f_t[:], ACT.Ln).then_inc(f_ln, 1)

            def step(base, i, period, h, q, has_attention):
                for u in range(len(UNITS)):
                    for c in range(2):
                        split(base + RING + 2 * u + c, i, period)
                    products(u, base + 2 * u, i, period, h, q)
                    if has_attention:
                        for job in STEP_ACT.get(u, ()):
                            attention(job, h - 1, 1 - q)

            forget_logits()
            step(HEADS0, None, 0, 0, 0, False)
            step(HEADS0 + N_HEAD, None, 0, 1, 1, True)
            with act.Fori(0, 3) as i:
                step(HEADS0 + 2 * N_HEAD, i, 2 * N_HEAD, i * 2 + 2, 0, True)
                step(HEADS0 + 3 * N_HEAD, i, 2 * N_HEAD, i * 2 + 3, 1, True)

            act.wait_ge(kv_out[0], 32 * (H // 2))
            for u in range(2 * PRE):
                for c in range(2):
                    split(GATES0 + RING + 2 * u + c)
                if u == 1:
                    add_bias(3 * KD - 1, 6 * KD - 2)
                chunk_used(act, GATES0 + 2 * u + 1)
                nc.scalar.activation(gate[u][:], banks[u % 2][:, 0:T], ACT.Exp, scale=-1.0).then_inc(gate_exp, 1)
                for job in LAST_ACT.get(u, ()):
                    attention(job, H - 1, (H - 1) % 2)

            act.wait_ge(state_out, 16 * H)
            act.wait_ge(state_p_out, 16 * H)
            act.wait_ge(lf_out, 32)
            act.wait_ge(ob_made, H)
            act.wait_ge(kv_out[1], 32 * (H // 2))
            for m in range(PRE):
                for c in range(2):
                    split(BRANCH0 + RING + 2 * m + c)
                act.wait_ge(sum_made, m + 1)
                copy(m_hi[:, m, :], gate[2 * m][:]).then_inc(m_hi_made, 1)
            with act.Fori(0, (KD - PRE) // 2) as i:
                for q in range(2):
                    m = i * 2 + (PRE + q)
                    for side in range(2):
                        for c in range(2):
                            split(MERGE0 + RING + 6 * q + 2 * side + c, i, 12)
                        chunk_used(act, at(MERGE0 + 6 * q + 2 * side + 1, i, 12))
                        act.wait_ge(m_made, m - 1)
                        nc.scalar.activation(gate[2 * q + side][:], banks[side][:, 0:T], ACT.Exp,
                                             scale=-1.0).then_inc(gate_exp, 1)
                    for c in range(2):
                        split(MERGE0 + RING + 6 * q + 4 + c, i, 12)
                    act.wait_ge(sum_made, m + 1)
                    copy(m_hi[:, m, :], gate[2 * q][:]).then_inc(m_hi_made, 1)
            with act.Fori(0, (UP0 - OUT0) // RING) as i:
                for n in range(RING):
                    split(OUT0 + RING + n, i, RING)

            def squares(n):
                for g in range(KD // 2):
                    act.wait_ge(centered, n * KD // 2 + g + 1)
                    if g >= 2:
                        act.wait_ge(sq_used, n * KD // 2 + g - 1)
                    nc.scalar.activation(ln_sq[g % 2][:], r[:, 2 * g:2 * g + 2, :], ACT.Square).then_inc(squared, 1)
                act.wait_ge(sq_used, (n + 1) * KD // 2)
                nc.scalar.activation(ln_var[:], banks[3][:, 0:T], ACT.Sqrt, bias=c_(C_EPS, 1),
                                     scale=1.0 / KD).then_inc(deviation, 1)

            squares(0)
            act.wait_ge(ln_factors, 3)
            for k in range(KD):
                act.wait_ge(normed, k // 2 + 1)
                if k >= 2:
                    act.wait_ge(u2_made, k - 1)
                nc.scalar.activation(u2_f[k % 2][:, 0:TP], r[:, k, 0:TP], ACT.Identity, bias=ln_c[:, k, 0:1],
                                     scale=ln_a[:, k, 0:1]).then_inc(u2_prompt, 1)
                act.wait_ge(u2_prompt, k + 1)
                act.wait_ge(u2_sample, k + 1)
                copy(u_hi[:, k, :], u2_f[k % 2][:]).then_inc(u2_hi_made, 1)
            for k in range(KD):
                nc.scalar.activation(r[:, k, :], r[:, k, :], ACT.Identity, bias=ln[:, 1, k:k + 1],
                                     scale=ln[:, 0, k:k + 1]).then_inc(x1_made, 1)

            act.wait_ge(ext_zero, 2)

            def up(base, first):
                with act.Fori(0, HALF // 2) as i:
                    for q in range(2):
                        n = i * 2 + (first + q)
                        b = base + 4 * q
                        a_bank = banks[4 + 2 * q]
                        for c in range(2):
                            split(b + RING + c, i, 8)
                        chunk_used(act, at(b + 1, i, 8))
                        act.wait_ge(hist, n + 1)
                        copy(a_ext[q][:, 2:2 + TP], a_bank[:, 0:TP]).then_inc(a_read, 1)
                        copy(histories(a_ext[q])[:, :, 2:], seqs(a_bank[:, TP:T])).then_inc(a_read, 1)
                        split(b + RING + 2, i, 8)
                        act.wait_ge(conv_made, n + 3)
                        nc.scalar.activation(conv[q][:, 0:EXT - 2], conv[q][:, 0:EXT - 2],
                                             ACT.Gelu_apprx_tanh).then_inc(gelu_made, 1)
                        split(b + RING + 3, i, 8)
                        act.wait_ge(hf_made, n * 2 + 6)
                        copy(h_hi[:, i * 2 + q, :], h_f[:]).then_inc(h_hi_made, 1)

            def down(base):
                if base != DOWN1:
                    with act.Fori(0, N_DOWN // RING) as i:
                        for n in range(RING):
                            split(base + RING + n, i, RING)
                else:
                    with act.Fori(0, N_DOWN // RING - 1) as i:
                        for n in range(RING):
                            split(base + RING + n, i, RING)

            up(UP0, 0)
            down(DOWN0)
            up(UP1, HALF)
            down(DOWN1)
            squares(1)
            for k in range(KD):
                act.wait_ge(normed, KD // 2 + k // 2 + 1)
                nc.scalar.activation(r[:, k, :], r[:, k, :], ACT.Identity, bias=ln[:, 3, k:k + 1],
                                     scale=ln[:, 2, k:k + 1]).then_inc(y_made, 1)

        @block.vector
        def _(dve):
            def split(base, i=None, period=0):
                if base >= CHUNKS:
                    return
                n, s = at(base, i, period), base % RING
                dve.wait_ge(hi_made, n + 1)
                nc.vector.tensor_tensor(w_lo[s][:], raw[s][:], w_hi[s][:].bitcast(F32),
                                        ALU.subtract).then_inc(lo_made, 1)

            dve.wait_ge(c_exp_made, 1)
            nc.vector.tensor_scalar(c_exp[:], c_exp[:], 1.0, None, ALU.add).then_inc(c_silu, 1)
            for n, m in enumerate((KD, 4 * KD)):
                nc.vector.tensor_scalar(b_ada[:, m:m + KD], b_ada[:, m:m + KD], 1.0, None, ALU.add)\
                    .then_inc(bias_one, 1)
            dve.wait_ge(c_silu, 1)
            nc.vector.reciprocal(c_exp[:], c_exp[:]).then_inc(c_silu, 1)
            dve.wait_ge(c_silu, 2)
            nc.vector.tensor_tensor(c_raw[:], c_raw[:], c_exp[:], ALU.mult).then_inc(c_silu, 1)
            for n in range(2):
                split(n)
            dve.wait_ge(c_hi_made, 1)
            nc.vector.tensor_tensor(c_parts[:, :, CROW:CROW + NSEQ], c_raw[:], c_parts[:, :, 0:NSEQ].bitcast(F32),
                                    ALU.subtract).then_inc(c_ready, 1)
            for n in range(2, RING):
                split(n)

            def stage(group, base, i=None, period=0):
                chunk_used(dve, at(base, i, period))
                dve.wait_ge(ada_turned, group + 1)
                nc.vector.tensor_copy(ada_rows[:], ADA_BANK[0:2 * CROW, 0:2 * P]).then_inc(ada_staged, 1)

            def make_u_prompt(g):
                dve.wait_ge(mod_made, g * 4 + 6)
                for q in range(2):
                    k = g * 2 + q
                    nc.vector.tensor_scalar(x[:, k, 0:TP], x[:, k, 0:TP], mod[:, k + KD, 0:1], mod[:, k, 0:1],
                                            ALU.mult, ALU.add).then_inc(u_prompt, 1)

            def conditioning(base, i, g, first):
                for half in range(2):
                    for c in range(4):
                        split(base + RING + 4 * half + c, i, 8)
                    stage(g * 2 + half, base + 4 * half + 3, i, 8)
                    if half == 0 and not first:
                        make_u_prompt(g - 1)

            conditioning(ADA0, None, 0, True)
            dve.wait_ge(x_in, 16)
            with dve.Fori(0, KD // 2 - 1) as i:
                conditioning(ADA0 + 8, i, i + 1, False)
            make_u_prompt(KD // 2 - 1)

            def forget_logits():
                nc.vector.memset(f_z[:], 0.0).then_inc(f_zero, 1)
                dve.wait_ge(small_in, 80)
                dve.wait_ge(f_zero, 1)
                dve.wait_ge(f_done, 1)
                nc.vector.tensor_tensor(f_z[:, 0:2, :], LOGF_BANK[:, 0:2 * H].rearrange("p (c h) -> p c h", c=2),
                                        rep(b_f[:], 2), ALU.add).then_inc(f_z_made, 1)
                nc.vector.tensor_tensor(f_z[0:NS, 2, :], LOGF_BANK[0:NS, 2 * H:3 * H], b_f[0:NS, :],
                                        ALU.add).then_inc(f_z_made, 1)
                dve.wait_ge(f_z_made, 2)
                nc.vector.scalar_tensor_tensor(out=f_t[:], in0=f_z[:], scalar=-1.0, in1=f_z[:], op0=ALU.mult,
                                               op1=ALU.max).then_inc(f_abs, 1)
                dve.wait_ge(f_exp, 1)
                nc.vector.tensor_scalar(f_t[:], f_t[:], 1.0, None, ALU.add).then_inc(f_one, 1)
                dve.wait_ge(f_ln, 1)
                nc.vector.scalar_tensor_tensor(out=lf[:], in0=f_z[:], scalar=0.0, in1=f_t[:], op0=ALU.min,
                                               op1=ALU.subtract).then_inc(lf_ready, 1)

            def products(u, base, i, period, h):
                if u in STAGE_AT:
                    stage(h * 4 + (KD + STAGE_AT[u]), base + 1, i, period)
                if u == 7:
                    dve.wait_ge(g_exp_made, h + 1)
                    nc.vector.tensor_scalar(g_exp[:], g_exp[:], 1.0, None, ALU.add).then_inc(g_one, 1)
                    dve.wait_ge(g_one, h + 1)
                    nc.vector.reciprocal(g_exp[:], g_exp[:]).then_inc(g_inv, 1)

            def attention(job, h, q):
                work = WORK[JOB[job] % 4] if job in JOB else None
                done = taken[JOB[job] % 4] if job in JOB else None
                if job in JOB:
                    is_written(dve, job, h)
                if job == "gather":
                    dve.wait_ge(lf_ready, 1)
                    dve.wait_ge(pages_in, 16 * NB * NPG)
                    nc.vector.tensor_copy(lf_h[:], lf[:, :, h]).then_inc(gathered, 1)
                    nc.vector.tensor_copy(lfp_h[:], lfp[:, :, h]).then_inc(gathered, 1)
                    dve.wait_ge(tab_in[q], (h - q) * 8 + 16)
                    dve.wait_ge(roped, 2 * h + 1)
                    nc.vector.tensor_tensor(q_dec[:], tiles[q]["qr"][:, TP:T], tab[q][:, T_CROSS:T_CROSS + NS],
                                            ALU.mult).then_inc(gathered, 1)
                elif job == "kr_rows":
                    for c in range(3):
                        n = P if c < 2 else NS
                        last = nc.vector.tensor_scalar(kr_rows[0:n, c, :], work[0:n, c * P:(c + 1) * P],
                                                       tab[q][0:n, T_KW + c:T_KW + c + 1], None, ALU.mult)
                    last.then_inc(done, 1)
                elif job == "scores":
                    settle(dve)
                    nc.vector.tensor_tensor_reduce(probs[:, 0:128], work[:, 0:128], c_(C_MASK + 128, 128), 1.0, MASKED,
                                                   ALU.add, ALU.max, smx[:, 0:1])
                    nc.vector.tensor_tensor_reduce(probs[:, 128:384], work[:, 128:384], c_(C_MASK, 256),
                                                   1.0, MASKED, ALU.add, ALU.max, smx[:, 1:2]).then_inc(done, 1)
                    is_taken(dve, "scores", h)
                    nc.vector.tensor_scalar(smx[:, 2:4], smx[:, 0:2], -1.0, None, ALU.mult).then_inc(neg_made, 1)
                elif job == "ret_scores":
                    nc.vector.tensor_tensor(att[:, 0:256], work[:, 0:256], tab[q][:, 0:256], ALU.mult)
                    nc.vector.tensor_tensor(att[:, 256:384], work[:, 256:384], tab[q][:, 0:128], ALU.mult)
                    nc.vector.tensor_tensor(att[0:NS, 384:448], work[0:NS, 384:448],
                                            tab[q][0:NS, T_SEQ:T_SEQ + NS], ALU.mult).then_inc(done, 1)
                elif job == "row_scores":
                    settle(dve)
                    nc.vector.tensor_tensor_reduce(row_p[:], work[0:NS, 0:T], c_(C_ROWMASK, T, NS), 1.0, MASKED,
                                                   ALU.add, ALU.max, srow[0:NS, 0:1]).then_inc(done, 1)
                    is_taken(dve, "row_scores", h)
                    nc.vector.tensor_scalar(srow[0:NS, 1:2], srow[0:NS, 0:1], -1.0, None,
                                            ALU.mult).then_inc(row_neg_made, 1)
                elif job == "normalise":
                    dve.wait_ge(exp_made, h + 1)
                    nc.vector.reciprocal(ssum[:, 2:4], ssum[:, 0:2]).then_inc(inv_made, 1)
                    dve.wait_ge(inv_made, h + 1)
                    nc.vector.tensor_scalar(probs[:, 0:128], probs[:, 0:128], ssum[:, 2:3], None, ALU.mult)
                    nc.vector.tensor_scalar(probs[:, 128:384], probs[:, 128:384], ssum[:, 3:4], None,
                                            ALU.mult).then_inc(probs_made, 1)
                elif job == "row_normalise":
                    dve.wait_ge(row_exp_made, h + 1)
                    nc.vector.reciprocal(srow[0:NS, 3:4], srow[0:NS, 2:3]).then_inc(row_inv_made, 1)
                    dve.wait_ge(row_inv_made, h + 1)
                    nc.vector.tensor_scalar(row_p[:], row_p[:], srow[0:NS, 3:4], None,
                                            ALU.mult).then_inc(row_probs_made, 1)
                elif job in ("state0", "state1"):
                    b = 4 * (job == "state1")
                    nc.vector.scalar_tensor_tensor(
                        out=state[:, b:b + 4, :], in0=state[:, b:b + 4, :], scalar=tab[q][:, T_DECAY:T_DECAY + 1],
                        in1=work[:].rearrange("p (b e) -> p b e", b=4), op0=ALU.mult, op1=ALU.add).then_inc(done, 1)
                elif job == "attend":
                    dve.wait_ge(oa_hi_made, h + 1)
                    nc.vector.tensor_tensor(oa_lo[:, h, :], work[:, 0:T], oa_hi[:, h, :].bitcast(F32),
                                            ALU.subtract).then_inc(done, 1)
                elif job == "center":
                    dve.wait_ge(sq_made, h + 1)
                    nc.vector.tensor_copy(o_cen[:], work[:, 0:T]).then_inc(done, 1)
                elif job == "deviation":
                    is_taken(dve, "variance", h)
                    nc.vector.reciprocal(o_var[:], o_var[:]).then_inc(o_rstd, 1)
                elif job == "ob_lo":
                    dve.wait_ge(ob_hi_made, h + 1)
                    nc.vector.tensor_tensor(ob_lo[:, h, :], o_cen[:], ob_hi[:, h, :].bitcast(F32),
                                            ALU.subtract).then_inc(ob_made, 1)

            def step(base, i, period, h, q, has_attention):
                for u in range(len(UNITS)):
                    for c in range(2):
                        split(base + RING + 2 * u + c, i, period)
                    products(u, base + 2 * u, i, period, h)
                    if has_attention:
                        for job in STEP_DVE.get(u, ()):
                            attention(job, h - 1, 1 - q)

            forget_logits()
            step(HEADS0, None, 0, 0, 0, False)
            step(HEADS0 + N_HEAD, None, 0, 1, 1, True)
            with dve.Fori(0, 3) as i:
                step(HEADS0 + 2 * N_HEAD, i, 2 * N_HEAD, i * 2 + 2, 0, True)
                step(HEADS0 + 3 * N_HEAD, i, 2 * N_HEAD, i * 2 + 3, 1, True)

            def sigmoid(slot, g):
                dve.wait_ge(gate_exp, g + 1)
                nc.vector.tensor_scalar(gate[slot][:], gate[slot][:], 1.0, None, ALU.add).then_inc(gate_one, 1)
                dve.wait_ge(gate_one, g + 1)
                nc.vector.reciprocal(gate[slot][:], gate[slot][:]).then_inc(gate_made, 1)

            def branch(slot, bank, n):
                dve.wait_ge(gate_made, n + 1)
                nc.vector.tensor_tensor(gate[slot][:], bank[:, 0:T], gate[slot][:], ALU.mult).then_inc(branch_read, 1)

            def merge(slot, m):
                dve.wait_ge(branch_read, m * 2 + 2)
                nc.vector.tensor_tensor(gate[slot][:], gate[slot][:], gate[slot + 1][:], ALU.add).then_inc(sum_made, 1)

            def merge_lo(slot, m):
                dve.wait_ge(m_hi_made, m + 1)
                nc.vector.tensor_tensor(m_lo[:, m, :], gate[slot][:], m_hi[:, m, :].bitcast(F32),
                                        ALU.subtract).then_inc(m_made, 1)

            for u in range(2 * PRE):
                for c in range(2):
                    split(GATES0 + RING + 2 * u + c)
                sigmoid(u, u)
                for job in LAST_DVE.get(u, ()):
                    attention(job, H - 1, (H - 1) % 2)
            for m in range(PRE):
                split(BRANCH0 + RING + 2 * m)
                chunk_used(dve, BRANCH0 + 2 * m)
                branch(2 * m, banks[3 + 2 * (m % 2)], 2 * m)
                chunk_used(dve, BRANCH0 + 2 * m + 1)
                branch(2 * m + 1, banks[4 + 2 * (m % 2)], 2 * m + 1)
                merge(2 * m, m)
                split(BRANCH0 + RING + 2 * m + 1)
                merge_lo(2 * m, m)
            with dve.Fori(0, (KD - PRE) // 2) as i:
                for q in range(2):
                    m = i * 2 + (PRE + q)
                    b = MERGE0 + 6 * q
                    for side in range(2):
                        for c in range(2):
                            split(b + RING + 2 * side + c, i, 12)
                        sigmoid(2 * q + side, m * 2 + side)
                    split(b + RING + 4, i, 12)
                    chunk_used(dve, at(b + 4, i, 12))
                    branch(2 * q, banks[3 + 2 * q], m * 2)
                    chunk_used(dve, at(b + 5, i, 12))
                    branch(2 * q + 1, banks[4 + 2 * q], m * 2 + 1)
                    merge(2 * q, m)
                    split(b + RING + 5, i, 12)
                    merge_lo(2 * q, m)

            def gated_residual(bank, before, gates, m, n):
                if not (isinstance(n, int) and n == 0):
                    dve.wait_ge(r_made, n)
                nc.vector.tensor_scalar(y_t[:, 0:TP], bank[:, 0:TP], gates[:, m, 0:1], None, ALU.mult)
                nc.vector.tensor_tensor(seqs(y_t[:, TP:T]), seqs(bank[:, TP:T]), per_seq(gates[:, m, 1:NSEQ]),
                                        ALU.mult).then_inc(proj_read, 1)
                dve.wait_ge(proj_read, n + 3)
                nc.vector.scalar_tensor_tensor(out=r[:, m, :], in0=before[:, m, :], scalar=ALPHA, in1=y_t[:],
                                               op0=ALU.mult, op1=ALU.add).then_inc(r_made, 1)

            gate1, gate2 = mod[:, 2 * KD:3 * KD, :], mod[:, 5 * KD:6 * KD, :]
            dve.wait_ge(x_again_in, 16)
            dve.wait_ge(mod_made, 6 * KD + 2)

            def out_tile(b, i, m, q):
                for c in range(2):
                    split(b + RING + c, i, RING)
                chunk_used(dve, at(b + 1, i, RING))
                gated_residual(banks[q], x_again, gate1, m, m)

            for q in range(2):
                out_tile(OUT0 + 2 * q, None, q, q)
            with dve.Fori(0, KD // 2 - 1) as i:
                for q in range(2):
                    out_tile(OUT0 + RING + 2 * q, i, i * 2 + (2 + q), q)

            def center_and_norm(n):
                dve.wait_ge(mean_done, n + 1)
                nc.vector.tensor_scalar(ln_mean[:], banks[2][:, 0:T], 1.0 / KD, None, ALU.mult).then_inc(mean_made, 1)
                dve.wait_ge(mean_made, n + 1)
                for g in range(KD // 2):
                    rows = r[:, 2 * g:2 * g + 2, :]
                    nc.vector.tensor_tensor(rows, rows, rep(ln_mean[:], 2), ALU.subtract).then_inc(centered, 1)
                dve.wait_ge(deviation, n + 1)
                nc.vector.reciprocal(ln_var[:], ln_var[:]).then_inc(rstd_made, 1)
                dve.wait_ge(rstd_made, n + 1)

            def norm(g):
                rows = r[:, 2 * g:2 * g + 2, :]
                nc.vector.tensor_tensor(rows, rows, rep(ln_var[:], 2), ALU.mult).then_inc(normed, 1)

            def u2_lo(k):
                dve.wait_ge(u2_hi_made, k + 1)
                nc.vector.tensor_tensor(u_lo[:, k, :], u2_f[k % 2][:], u_hi[:, k, :].bitcast(F32),
                                        ALU.subtract).then_inc(u2_made, 1)

            center_and_norm(0)
            norm(0)
            for g in range(1, KD // 2):
                norm(g)
                u2_lo(2 * g - 2)
                u2_lo(2 * g - 1)
            u2_lo(KD - 2)
            u2_lo(KD - 1)
            dve.wait_ge(ffn_in, 32)

            def up(base, first):
                with dve.Fori(0, HALF // 2) as i:
                    for q in range(2):
                        n = i * 2 + (first + q)
                        b = base + 4 * q
                        b_bank = banks[5 + 2 * q]
                        e, w = a_ext[q], EXT - 2
                        for c in range(2):
                            split(b + RING + c, i, 8)
                        dve.wait_ge(a_read, n * 2 + 6)
                        dve.wait_ge(hist, n + 1)
                        nc.vector.tensor_scalar(conv[q][:, 0:w], e[:, 2:2 + w], w_conv[:, n, 2:3], w_conv[:, n, 3:4],
                                                ALU.mult, ALU.add).then_inc(conv_step, 1)
                        dve.wait_ge(conv_step, n * 2 + 1)
                        nc.vector.scalar_tensor_tensor(out=conv[q][:, 0:w], in0=e[:, 1:1 + w],
                                                       scalar=w_conv[:, n, 1:2], in1=conv[q][:, 0:w],
                                                       op0=ALU.mult, op1=ALU.add).then_inc(conv_step, 1)
                        dve.wait_ge(conv_step, n * 2 + 2)
                        nc.vector.scalar_tensor_tensor(out=conv[q][:, 0:w], in0=e[:, 0:w],
                                                       scalar=w_conv[:, n, 0:1], in1=conv[q][:, 0:w],
                                                       op0=ALU.mult, op1=ALU.add).then_inc(conv_made, 1)
                        split(b + RING + 2, i, 8)
                        chunk_used(dve, at(b + 3, i, 8))
                        dve.wait_ge(gelu_made, n + 1)
                        nc.vector.tensor_tensor(h_f[:, 0:TP], conv[q][:, 0:TP], b_bank[:, 0:TP],
                                                ALU.mult).then_inc(hf_made, 1)
                        nc.vector.tensor_tensor(seqs(h_f[:, TP:T]), histories(conv[q])[:, :, 0:TS],
                                                seqs(b_bank[:, TP:T]), ALU.mult).then_inc(hf_made, 1)
                        split(b + RING + 3, i, 8)
                        dve.wait_ge(h_hi_made, n + 1)
                        dve.wait_ge(hf_made, n * 2 + 6)
                        nc.vector.tensor_tensor(h_lo[:, i * 2 + q, :], h_f[:],
                                                h_hi[:, i * 2 + q, :].bitcast(F32), ALU.subtract).then_inc(h_made, 1)

            def down(base, half):
                last = 4 if base == DOWN1 else 0
                turns = N_DOWN // 12

                def body(i, final):
                    for j in range(4):
                        for c in range(3):
                            n = base + 3 * j + c
                            if final:
                                split(n + RING + 12 * (turns - 1))
                            else:
                                split(n + RING, i, 12)
                        m = (4 * (turns - 1) if final else i * 4) + j
                        done = KD * (1 + half)
                        chunk_used(dve, base + 12 * (turns - 1) + 3 * j + 2 if final else at(base + 3 * j + 2, i, 12))
                        bank = banks[j % 2]
                        if half == 0:
                            dve.wait_ge(x1_made, KD)
                            gated_residual(bank, r, gate2, m, m + done)
                        else:
                            dve.wait_ge(r_made, m + done)
                            nc.vector.scalar_tensor_tensor(out=r[:, m, 0:TP], in0=bank[:, 0:TP],
                                                           scalar=gate2[:, m, 0:1], in1=r[:, m, 0:TP],
                                                           op0=ALU.mult, op1=ALU.add)
                            nc.vector.tensor_tensor(seqs(y_t[:, TP:T]), seqs(bank[:, TP:T]),
                                                    per_seq(gate2[:, m, 1:NSEQ]), ALU.mult).then_inc(proj_read, 1)
                            dve.wait_ge(proj_read, m + (done + 3))
                            nc.vector.tensor_tensor(r[:, m, TP:T], r[:, m, TP:T], y_t[:, TP:T],
                                                    ALU.add).then_inc(r_made, 1)

                with dve.Fori(0, turns - (half == 1)) as i:
                    body(i, False)
                if half == 1:
                    body(None, True)

            up(UP0, 0)
            down(DOWN0, 0)
            up(UP1, HALF)
            down(DOWN1, 1)
            dve.wait_ge(summed, 2 * KD + 2)
            center_and_norm(1)
            for g in range(KD // 2):
                norm(g)

        @block.tensor
        def _(pe):
            ident = c_(C_IDENT, P)

            def mm(out, lhsT, rhs, start=False, stop=False):
                return nc.tensor.matmul(out, lhsT, rhs, start=start, stop=stop, skip_group_check=True)

            def chunk(out, x_hi, x_lo, k0, base, i=None, period=0, blocks=CB, first=False, last=False):
                s = base % RING
                pe.wait_ge(lo_made, at(base + 1, i, period))
                for b in range(blocks):
                    k = k0 + b
                    mm(out, w_hi[s][:, b, :], x_lo[:, k, :], start=first and b == 0)
                    mm(out, w_hi[s][:, b, :], x_hi[:, k, :])
                    ins = mm(out, w_lo[s][:, b, :], x_hi[:, k, :], stop=last and b == blocks - 1)
                ins.then_inc(used, 1)

            def tile(out, x_hi, x_lo, base, i=None, period=0):
                chunk(out, x_hi, x_lo, 0, base, i, period, first=True)
                chunk(out, x_hi, x_lo, CB, base + 1, i, period, last=True)

            def ada(c, base, i, period, group):
                if c == 0:
                    pe.wait_ge(ada_staged, group + 1)
                s = base % RING
                pe.wait_ge(lo_made, at(base + 1, i, period))
                for b in range(CB // 2):
                    k = c * (CB // 2) + b
                    rows = c_hl[:, k * 2 * CROW:k * 2 * CROW + P]
                    for w in (w_hi, w_lo):
                        ins = mm(ADA_BANK[:, 0:2 * P], rows, w[s][:, 2 * b:2 * b + 2, :].rearrange("p k c -> p (k c)"),
                                 start=k == 0 and w is w_hi, stop=k == KD - 1 and w is w_lo)
                ins.then_inc(used, 1)

            def turn(group):
                pe.wait_ge(ada_staged, group + 2)
                pe.wait_ge(mod_made, group * 2 + 2)
                for j in range(2):
                    ins = mm(MOD_BANK[:, CROW * j:CROW * j + NSEQ], ada_rows[:, j * P:(j + 1) * P],
                             c_(C_SUM, NSEQ, 2 * CROW), start=True, stop=True)
                ins.then_inc(ada_turned, 1)

            def conditioning(base, i, g, first):
                for half in range(2):
                    for c in range(4):
                        ada(c, base + 4 * half + c, i, 8, g * 2 + half)
                        if c == 0 and not (first and half == 0):
                            turn(g * 2 + (half - 1))

            pe.wait_ge(c_ready, 2)
            pe.wait_ge(small_in, 80)
            conditioning(ADA0, None, 0, True)
            with pe.Fori(0, KD // 2 - 1) as i:
                conditioning(ADA0 + 8, i, i + 1, False)
            turn(KD - 1)

            pe.wait_ge(u_lo_made, KD)
            pe.wait_ge(mod_made, 2 * KD + 2)
            for c in range(3):
                n = P if c < 2 else NS
                for k in range(KD):
                    ins = mm(LOGF_BANK[0:n, c * H:(c + 1) * H], x[:, k, c * P:c * P + n], w_f[:, k, :],
                             start=k == 0, stop=k == KD - 1)
            ins.then_inc(f_done, 1)

            def attention(job, h, q):
                kk = JOB[job]
                w = WORK[kk % 4]
                t = tiles[q]
                pe.wait_ge(taken[kk % 4], 4 * h + (kk // 4 + 1))
                if job in ("v_rows", "kr_rows", "vr_rows"):
                    if job == "v_rows":
                        tile_is_read(pe, "va", h)
                    if job == "kr_rows":
                        pe.wait_ge(roped, 2 * h + 2)
                    src = t[{"v_rows": "va", "kr_rows": "kr", "vr_rows": "vr"}[job]]
                    for c in range(3):
                        n = P if c < 2 else NS
                        ins = nc.tensor.transpose(w[0:n, c * P:(c + 1) * P], src[:, c * P:c * P + n], ident)
                elif job == "scores":
                    pe.wait_ge(gathered, 3 * h + 3)
                    lf0, lf1 = (lf_h[:, c:c + 1].to_broadcast([P, P]) for c in range(2))
                    mm(w[:, 0:128], t["qa"][:, 0:128], t["ka"][:, 0:128], start=True)
                    mm(w[:, 0:128], lf0, c_(C_NEGTRI, 128))
                    mm(w[:, 128:384], t["qa"][:, 128:256], t["ka"][:, 0:256])
                    mm(w[:, 128:384], lf0, c_(C_NEGTRI, 256))
                    ins = mm(w[:, 256:384], lf1, c_(C_NEGTRI, 128), stop=True)
                elif job == "past_scores":
                    pe.wait_ge(k_in, (h + 1) * (16 * NB * NPG))
                    past = lfp_h[:].rearrange("p (b g) -> p g b", g=NPG)
                    sides = [w[:, g * NS:(g + 1) * NS].rearrange("p (b t) -> p b t", b=NB) for g in range(NPG)]
                    mm(sides[0], c_(C_AFTER, P), per_seq(past[:, 0, :]), start=True)
                    mm(sides[0], c_(C_ONE, 1).to_broadcast([P, P]), per_seq(past[:, 1, :]))
                    mm(sides[1], c_(C_AFTER, P), per_seq(past[:, 1, :]))
                    for b in range(NB):
                        for g in range(NPG):
                            ins = mm(sides[g][:, b, :], kv[:, b * NPG + g, 0:P],
                                     t["qa"][:, TP + b * TS:TP + (b + 1) * TS], stop=b == NB - 1 and g == NPG - 1)
                elif job == "ret_scores":
                    mm(w[:, 0:256], t["kr"][:, 0:128], t["qr"][:, 0:256], start=True)
                    mm(w[:, 256:384], t["kr"][:, 128:256], t["qr"][:, 128:256])
                    ins = mm(w[0:NS, 384:448], t["kr"][:, TP:T], t["qr"][:, TP:T], stop=True)
                elif job == "row_scores":
                    is_taken(pe, "past_scores", h)
                    settle(pe)
                    for g in range(NPG):
                        nc.tensor.transpose(w[0:NS, g * P:(g + 1) * P], past_t[:, g * NS:(g + 1) * NS], ident)
                    mm(w[0:NS, TP:T], t["qa"][:, TP:T], t["ka"][:, TP:T], start=True)
                    ins = mm(w[0:NS, TP:T], lf_h[0:NS, 2:3].to_broadcast([NS, NS]), c_(C_NEGTRI_SEQ, NS, NS),
                             stop=True)
                elif job == "ret_state":
                    is_taken(pe, "kr_rows", h)
                    is_taken(pe, "vr_rows", h)
                    mm(w[:, 0:DH], kr_rows[:, 0, :], vr_rows[:, 0, :], start=True)
                    ins = mm(w[:, 0:DH], kr_rows[:, 1, :], vr_rows[:, 1, :], stop=True)
                elif job == "probs_t":
                    pe.wait_ge(probs_made, h + 1)
                    for c in range(3):
                        ins = nc.tensor.transpose(w[:, c * P:(c + 1) * P], probs[:, c * P:(c + 1) * P], ident)
                elif job == "ret_out":
                    is_taken(pe, "ret_scores", h)
                    pe.wait_ge(state_in, (h + 1) * 16)
                    mm(w[:, 0:256], vr_rows[:, 0, :], att[:, 0:256], start=True)
                    mm(w[:, 128:256], vr_rows[:, 1, :], att[:, 256:384])
                    mm(w[:, TP:T], vr_rows[0:NS, 2, :], att[0:NS, 384:448])
                    for b in range(NB):
                        ins = mm(w[:, TP + b * TS:TP + (b + 1) * TS], state[:, b, :], q_dec[:, b * TS:(b + 1) * TS],
                                 stop=b == NB - 1)
                elif job == "row_probs_t":
                    pe.wait_ge(row_probs_made, h + 1)
                    settle(pe)
                    for g in range(NPG):
                        nc.tensor.transpose(w[:, g * NS:(g + 1) * NS], row_p[:, g * P:(g + 1) * P],
                                            c_(C_IDENT, NS, NS))
                    ins = nc.tensor.transpose(w[0:NS, 128:192], row_p[:, TP:T], c_(C_IDENT, NS, NS))
                elif job in ("state0", "state1"):
                    pe.wait_ge(v_seq_made, h + 1)
                    b = 4 * (job == "state1")
                    ins = mm(w[:].rearrange("p (b e) -> p b e", b=4), kr_rows[0:NS, 2, :], v_seq[:, b:b + 4, :],
                             start=True, stop=True)
                elif job == "attend":
                    is_taken(pe, "probs_t", h)
                    is_taken(pe, "row_probs_t", h)
                    is_taken(pe, "v_rows", h)
                    pe.wait_ge(v_in, (h + 1) * (16 * NB * NPG))
                    mm(w[:, 0:256], v_rows[:, 0, :], probs_t[:, 0:256], start=True)
                    mm(w[:, 128:256], v_rows[:, 1, :], probs_t[:, 256:384])
                    mm(w[:, TP:T], v_rows[0:NS, 2, :], row_pt[0:NS, 128:192])
                    for b in range(NB):
                        for g in range(NPG):
                            c = g * NS + b * TS
                            ins = mm(w[:, TP + b * TS:TP + (b + 1) * TS], kv[:, b * NPG + g, P:2 * P],
                                     row_pt[:, c:c + TS], stop=b == NB - 1 and g == NPG - 1)
                elif job == "center":
                    is_taken(pe, "ret_out", h)
                    ins = mm(w[:, 0:T], c_(C_CENTER, P), o_ret[:], start=True, stop=True)
                elif job == "variance":
                    pe.wait_ge(sq_made, h + 1)
                    ins = mm(w[:, 0:T], c_(C_MEAN, P), o_sq, start=True, stop=True)
                ins.then_inc(written[kk % 4], 1)

            def step(base, i, period, h, q, has_attention):
                for u, name in enumerate(UNITS):
                    b = base + 2 * u
                    if name == "ada":
                        n_ada = sum(x == "ada" for x in UNITS[:u])
                        for c in range(2):
                            ada(2 * (n_ada % 2) + c, b + c, i, period, h * 4 + (KD + n_ada // 2))
                    else:
                        g = GEMMS.index(name)
                        if g >= 2:
                            tile_is_read(pe, GEMMS[g - 2], h)
                        elif not (isinstance(h, int) and h == 0):
                            tile_is_read(pe, GEMMS[g + 5], h - 1)
                        tile(banks[(q + g) % 2][:, 0:T], u_hi, u_lo, b, i, period)
                    if u in TURN_AT:
                        j = TURN_AT[u] - 4 * (u == 0)
                        if isinstance(h, int) and h == 0 and j == 0:
                            pe.wait_ge(f_z_made, 2)
                        if not (isinstance(h, int) and 4 * h + j < 0):
                            turn(h * 4 + (KD + j))
                    if has_attention:
                        for job in STEP_PE.get(u, ()):
                            attention(job, h - 1, 1 - q)

            step(HEADS0, None, 0, 0, 0, False)
            step(HEADS0 + N_HEAD, None, 0, 1, 1, True)
            with pe.Fori(0, 3) as i:
                step(HEADS0 + 2 * N_HEAD, i, 2 * N_HEAD, i * 2 + 2, 0, True)
                step(HEADS0 + 3 * N_HEAD, i, 2 * N_HEAD, i * 2 + 3, 1, True)

            for u in range(2 * PRE):
                if u < 2:
                    tile_is_read(pe, GEMMS[5 + u], H - 1)
                else:
                    pe.wait_ge(gate_exp, u - 1)
                tile(banks[u % 2][:, 0:T], u_hi, u_lo, GATES0 + 2 * u)
                if u == 0:
                    turn(3 * KD - 1)
                for job in LAST_PE.get(u, ()):
                    attention(job, H - 1, (H - 1) % 2)

            pe.wait_ge(ob_made, H)
            for w in range(4):
                pe.wait_ge(taken[w], 4 * H + 1)

            def branches(base, i, period, m, q):
                for side, (o_hi, o_lo) in enumerate(((oa_hi, oa_lo), (ob_hi, ob_lo))):
                    if not isinstance(m, int) or m >= 2:
                        pe.wait_ge(branch_read, m * 2 + (side - 3))
                    chunk(banks[3 + 2 * q + side][:, 0:T], o_hi, o_lo, 0, base + side, i, period,
                          first=True, last=True)

            for m in range(PRE):
                branches(BRANCH0 + 2 * m, None, 0, m, m % 2)
            with pe.Fori(0, (KD - PRE) // 2) as i:
                for q in range(2):
                    m = i * 2 + (PRE + q)
                    for side in range(2):
                        pe.wait_ge(gate_exp, m * 2 + (side - 1))
                        tile(banks[side][:, 0:T], u_hi, u_lo, MERGE0 + 6 * q + 2 * side, i, 12)
                    branches(MERGE0 + 6 * q + 4, i, 12, m, q)

            pe.wait_ge(m_made, KD)
            pe.wait_ge(gate_exp, 2 * KD)
            with pe.Fori(0, KD // 2) as i:
                for q in range(2):
                    pe.wait_ge(proj_read, i * 2 + (q + 1))
                    tile(banks[q][:, 0:T], m_hi, m_lo, OUT0 + 2 * q, i, RING)

            def layer_norm(n):
                pe.wait_ge(summed, n * (KD + 1) + KD + 1)
                mm(banks[2][:, 0:T], c_(C_MEAN, P), ln_sum[:], start=True, stop=True).then_inc(mean_done, 1)
                for g in range(KD // 2):
                    pe.wait_ge(squared, n * KD // 2 + g + 1)
                    for j in range(2):
                        ins = mm(banks[3][:, 0:T], c_(C_MEAN, P), ln_sq[g % 2][:, j, :], start=g == 0 and j == 0,
                                 stop=g == KD // 2 - 1 and j == 1)
                    ins.then_inc(sq_used, 1)

            layer_norm(0)
            pe.wait_ge(branch_read, 2 * KD)

            def up(base, first):
                with pe.Fori(0, HALF // 2) as i:
                    for q in range(2):
                        n = i * 2 + (first + q)
                        b = base + 4 * q
                        pe.wait_ge(a_read, n * 2 + 2)
                        tile(banks[4 + 2 * q][:, 0:T], u_hi, u_lo, b, i, 8)
                        pe.wait_ge(hf_made, n * 2 + 2)
                        tile(banks[5 + 2 * q][:, 0:T], u_hi, u_lo, b + 2, i, 8)

            def down(base, half):
                pe.wait_ge(h_made, HALF * (1 + half))
                with pe.Fori(0, KD // 4) as i:
                    for j in range(4):
                        pe.wait_ge(proj_read, i * 4 + (j + KD * (1 + half) + 1))
                        k0 = 0
                        for c, blocks in enumerate(DOWN_BLOCKS):
                            chunk(banks[j % 2][:, 0:T], h_hi, h_lo, k0, base + 3 * j + c, i, 12, blocks,
                                  first=c == 0, last=c == 2)
                            k0 += blocks

            pe.wait_ge(u2_made, KD)
            up(UP0, 0)
            down(DOWN0, 0)
            up(UP1, HALF)
            down(DOWN1, 1)
            layer_norm(1)


def tables():
    j, s = np.arange(P)[:, None], np.arange(P)[None, :]
    f = np.zeros((P, N_CONST), np.float32)
    f[:, C_IDENT:C_IDENT + P] = np.eye(P)
    f[:, C_CENTER:C_CENTER + P] = np.eye(P) - 1.0 / P
    f[:, C_MEAN:C_MEAN + P] = 1.0 / P
    f[:, C_AFTER:C_AFTER + P] = j > s
    f[:, C_NEGTRI:C_NEGTRI + P] = -1.0 * (j <= s)
    f[:, C_NEGTRI + P:C_NEGTRI + 2 * P] = -1.0
    f[:, C_MASK + P:C_MASK + 2 * P] = np.where(s <= j, 0.0, MASKED)
    n = np.arange(NS)
    same = n[:, None] // TS == n[None, :] // TS
    f[:NS, C_ROWMASK + TP:C_ROWMASK + T] = np.where(same & (n[None, :] <= n[:, None]), 0.0, MASKED)
    f[:NS, C_NEGTRI_SEQ:C_NEGTRI_SEQ + NS] = -1.0 * (same & (n[:, None] <= n[None, :]))
    f[:NS, C_SEQ:C_SEQ + NB] = n[:, None] // TS == np.arange(NB)[None, :]
    f[:, C_EPS], f[:, C_ONE] = EPS, 1.0
    r = np.arange(2 * CROW)[:, None]
    f[:2 * CROW, C_SUM:C_SUM + NSEQ] = r % CROW == np.arange(NSEQ)[None, :]
    t = np.zeros((H, P, N_TAB), np.float32)
    for h in range(H):
        g = 1.0 - 2.0 ** (-5.0 - h)
        i = np.arange(TP)[None, :]
        t[h, :, 0:TP] = np.where(i >= j, g ** np.maximum(i - j, 0).astype(np.float64), 0.0)
        t[h, :NS, T_SEQ:T_SEQ + NS] = np.where(same & (n[None, :] >= n[:, None]),
                                               g ** np.maximum(n[None, :] - n[:, None], 0).astype(np.float64), 0.0)
        t[h, :, T_CROSS:T_CROSS + NS] = g ** (n % TS + 1.0)[None, :]
        t[h, :, T_KW] = g ** (TP - 1.0 - np.arange(P))
        t[h, :, T_KW + 1] = g ** (P - 1.0 - np.arange(P))
        t[h, :, T_KW + 2] = g ** (TS - 1.0 - np.arange(P) % TS)
        t[h, :, T_DECAY] = g ** TS
    half = DH // 2
    inv = (10000.0 ** (-np.arange(half, dtype=np.float32) / half)).astype(np.float32)
    pos = np.concatenate([np.arange(TP), NPG * PAGE + np.tile(np.arange(TS), NB)]).astype(np.float32)
    ang = (inv[:, None] * pos[None, :]).astype(np.float32)
    cs = np.zeros((P, 2, T), np.float32)
    cs[:half, 0], cs[half:, 0] = np.cos(ang), np.cos(ang)
    cs[:half, 1], cs[half:, 1] = -np.sin(ang), np.sin(ang)
    return f, t, cs


def by_tile(w, n_tiles):
    k = w.shape[0]
    t = w.reshape(k // CW, CB, P, n_tiles, P).transpose(3, 0, 2, 1, 4)
    return t.reshape(n_tiles, k // CW, P, CW)


def by_feature(v, n):
    return np.ascontiguousarray(np.swapaxes(v.reshape((n, P) + v.shape[1:]), 0, 1))


def weight_stream(w_ada, w_in, w_pa, w_pb, w_o, w_up, w_down):
    w = np.zeros((CHUNKS, P, CW), np.float32)
    ada = w_ada.reshape(N_GROUP, CB // 2, P, 3 * KD, 2 * P).transpose(3, 0, 2, 1, 4).reshape(3 * KD, N_GROUP, P, CW)
    w[ADA0:HEADS0] = np.stack([ada[0:KD // 2], ada[KD // 2:KD]], 1).reshape(-1, P, CW)
    rest = ada[KD:].reshape(-1, 2, P, CW)
    edges = {"qa": 0, "ka": 1024, "va": 2048, "qr": 3080, "kr": 4104, "vr": 5128, "gr": 6152}
    inp = {u: by_tile(w_in[:, c:c + H * DH], H) for u, c in edges.items()}
    gates = [by_tile(w_in[:, c:c + D], KD) for c in (7176, 7176 + D)]
    n, m = HEADS0, 0
    for h in range(H):
        for u in UNITS:
            if u == "ada":
                w[n:n + 2] = rest[m]
                m += 1
            else:
                w[n:n + 2] = inp[u][h]
            n += 2
    branch = [by_tile(w_pa, KD), by_tile(w_pb, KD)]
    for m in range(PRE):
        for side in range(2):
            w[n:n + 2] = gates[side][m]
            n += 2
    for m in range(PRE):
        for side in range(2):
            w[n] = branch[side][m, 0]
            n += 1
    for m in range(PRE, KD):
        for side in range(2):
            w[n:n + 2] = gates[side][m]
            n += 2
        for side in range(2):
            w[n] = branch[side][m, 0]
            n += 1
    w[OUT0:UP0] = by_tile(w_o, KD).reshape(-1, P, CW)
    up = by_tile(w_up, 2 * KF)
    both = np.stack([up[:KF], up[KF:]], 1)
    down = w_down.reshape(2, HALF, P, KD, P).transpose(0, 3, 2, 1, 4).reshape(2, KD, P, HALF * P)
    for half, (u0, d0) in enumerate(((UP0, DOWN0), (UP1, DOWN1))):
        w[u0:u0 + N_UP] = both[half * HALF:(half + 1) * HALF].reshape(-1, P, CW)
        for c, blocks in enumerate(DOWN_BLOCKS):
            w[d0 + c:d0 + N_DOWN:3, :, 0:blocks * P] = down[half][:, :, c * CW:c * CW + blocks * P]
    return w


def kernel(**inputs):
    import concourse.bacc as bacc
    from concourse.bass_utils import run_bass_kernel_spmd

    v = {k: np.asarray(x) for k, x in inputs.items()}
    pool = v["cache_k"].shape[1]
    consts, tab, cossin = tables()
    kc = v["cache_k"][0].transpose(0, 2, 3, 1)
    vc = v["cache_v"][0].transpose(0, 2, 1, 3)
    arrays = {
        "w": weight_stream(*(v[n][0] for n in ("w_ada", "w_in", "w_pa", "w_pb", "w_o", "w_up", "w_down"))),
        "x": by_feature(np.concatenate([v["x_prompt"][0], v["x_sample"].reshape(NS, D)]).T, KD),
        "c": by_feature(np.concatenate([v["c_prompt"], v["c_sample"]]).T, KD),
        "b_ada": by_feature(v["b_ada"][0], 6 * KD),
        "consts": consts, "tab": tab, "cossin": cossin,
        "w_f": by_feature(v["w_in"][0][:, 3072:3072 + H], KD),
        "b_f": v["b_f"][0],
        "ln": np.stack([by_feature(v[n][0], KD) for n in ("ln1_g", "ln1_b", "ln2_g", "ln2_b")], 1),
        "pages": v["page_table"].reshape(1, NB * NPG),
        "cache_kv": np.stack([kc, vc], 2),
        "cache_lf": v["cache_logf"][0],
        "state": v["state_ret"][0],
        "w_conv": np.concatenate([by_feature(v["conv_w"][0].T, KF), by_feature(v["conv_b"][0], KF)[:, :, None]], 2),
        "s_conv": by_feature(v["state_conv"][0].transpose(2, 0, 1), KF),
    }
    outs = {"y": (P, KD, T), "kv_new": (2, H, DH, T), "lf_prompt": (TP, H), "lf_sample": (NS, H),
            "ret_prompt": (H, DH, DH), "ret_sample": (NB, H, DH, DH), "conv": (P, KF, NSEQ, 2)}
    nc = bacc.Bacc("TRN2", target_bir_lowering=False, num_devices=1)
    arrays = {f"in_{n}": np.ascontiguousarray(x) for n, x in arrays.items()}
    args = {n[3:]: nc.dram_tensor(n, x.shape, mybir.dt.from_np(x.dtype), kind="ExternalInput").ap()
            for n, x in arrays.items()}
    args |= {n: nc.dram_tensor(f"out_{n}", s, F32, kind="ExternalOutput").ap() for n, s in outs.items()}
    build(nc, args)
    got = run_bass_kernel_spmd(nc, [arrays], core_ids=[0]).results[0]
    y = got["out_y"].transpose(2, 1, 0).reshape(T, D)
    kv_new = got["out_kv_new"].transpose(0, 3, 1, 2)
    cv = got["out_conv"].transpose(2, 3, 1, 0).reshape(NSEQ, 2, DFF)
    c = np.ascontiguousarray
    return (c(y[:TP][None]), c(y[TP:].reshape(NB, TS, D)),
            c(kv_new[0, :TP][None, None]), c(kv_new[1, :TP][None, None]), c(got["out_lf_prompt"][None, None]),
            c(got["out_ret_prompt"][None, None]), c(cv[:1][None]),
            c(kv_new[0, TP:].reshape(1, NB, TS, H, DH)), c(kv_new[1, TP:].reshape(1, NB, TS, H, DH)),
            c(got["out_lf_sample"].reshape(1, NB, TS, H)), c(got["out_ret_sample"][None]), c(cv[1:][None]))
```

```python
from contextlib import ExitStack

import numpy as np

import concourse.bass as bass
from concourse import mybir

ALU = mybir.AluOpType
ACT = mybir.ActivationFunctionType
F32 = mybir.dt.float32
F32R = mybir.dt.float32r

P = 128
D = 2048
KD = D // P
TP = 256
NB, TS = 8, 8
NS = NB * TS
T = TP + NS
H = 8
DH = 128
PAGE = 128
NPG = 2
DFF = 5632
KF = DFF // P
HALF = KF // 2
NSEQ = 1 + NB
ALPHA = 2.0 ** 0.25
EPS = 1e-5
MASKED = -1e30

CB = 8
CW = CB * P
RING = 4
CROW = 10
N_GROUP = 4
UNITS = ["qr", "ada", "kr", "ada", "vr", "ada", "gr", "ada", "qa", "ada", "ka", "ada", "va", "ada", "ada"]
GEMMS = [u for u in UNITS if u != "ada"]
PRE = 4
N_ADA = 2 * 2 * KD
N_HEAD = 2 * len(UNITS)
ADA0 = 0
HEADS0 = ADA0 + N_ADA
GATES0 = HEADS0 + H * N_HEAD
BRANCH0 = GATES0 + 4 * PRE
MERGE0 = BRANCH0 + 2 * PRE
OUT0 = MERGE0 + 6 * (KD - PRE)
UP0 = OUT0 + 2 * KD
N_UP, N_DOWN = 4 * HALF, 3 * KD
DOWN0 = UP0 + N_UP
UP1 = DOWN0 + N_DOWN
DOWN1 = UP1 + N_UP
CHUNKS = DOWN1 + N_DOWN
DOWN_BLOCKS = [8, 8, HALF - 16]

JOBS = ["v_rows", "kr_rows", "vr_rows", "scores", "past_scores", "ret_scores", "row_scores", "ret_state",
        "probs_t", "ret_out", "row_probs_t", "center", "variance", "state0", "state1", "attend"]
JOB = {name: k for k, name in enumerate(JOBS)}
STEP_PE = {0: ["v_rows", "kr_rows"], 1: ["vr_rows", "scores"], 3: ["ret_scores"], 4: ["row_scores"],
           5: ["ret_state"], 6: ["probs_t"], 8: ["center", "row_probs_t"], 10: ["variance", "state0"],
           11: ["state1"]}
WITHIN = {2: "past_scores", 6: "ret_out", 12: "attend"}
STEP_ACT = {0: ["v_rows"], 1: ["vr_rows"], 2: ["past_scores"], 3: ["exp"], 5: ["row_exp", "ret_state"],
            6: ["ret_out", "probs_t"], 8: ["center", "row_probs_t"], 10: ["variance"], 12: ["attend"],
            14: ["ob_hi"]}
STEP_DVE = {0: ["kr_rows"], 2: ["scores"], 3: ["ret_scores"], 4: ["row_scores", "normalise"],
            6: ["row_normalise"], 8: ["center"], 10: ["deviation"], 11: ["state0"], 12: ["state1", "attend"],
            14: ["ob_lo"]}
STAGE_AT = {3: 0, 7: 1, 11: 2, 14: 3}
TURN_AT = {4: 0, 8: 1, 12: 2, 0: 3}
BIAS_AT = {5: 0, 9: 1, 13: 2, 1: 3}
LAST_PE = {0: ["v_rows", "kr_rows", "vr_rows"], 1: ["scores"], 2: ["ret_scores"], 3: ["row_scores", "ret_state"],
           4: ["probs_t"], 5: ["row_probs_t", "center", "state0", "state1", "variance"]}
LAST_WITHIN = {2: "past_scores", 4: "ret_out", 6: "attend"}
LAST_ACT = {0: ["v_rows", "vr_rows"], 2: ["past_scores", "exp"], 3: ["row_exp", "ret_state"],
            4: ["ret_out", "probs_t"], 5: ["row_probs_t", "center", "variance"], 6: ["attend", "ob_hi"]}
LAST_DVE = {0: ["kr_rows"], 1: ["scores"], 2: ["ret_scores", "normalise"], 3: ["row_scores"],
            4: ["row_normalise"], 5: ["center", "state0", "state1", "deviation"], 6: ["attend", "ob_lo"]}

SPLIT_AFTER = {11: 0, 13: 1}
KEEP_WARM = 50
NORM_ON_POOL = 12

C_SUM = 0
C_EPS, C_ONE = 10, 11
N_FIRST = 16
C_IDENT, C_CENTER, C_MEAN, C_AFTER = 16, 144, 272, 400
C_NEGTRI = 528
C_MASK = 784
C_ROWMASK = 1040
C_NEGTRI_SEQ = 1360
C_SEQ = 1424
N_CONST = 1432
T_SEQ, T_CROSS, T_KW, T_DECAY = 256, 320, 384, 387
N_TAB = 388


def at(base, i=None, period=0):
    return base if i is None else base + i * period


def build(nc, a):
    sb_base = 16512
    top = [sb_base]
    limit = nc.sbuf_usable_end

    def place(name, shape, dt=F32, offset=None):
        size = int(np.prod(shape[1:])) * 4
        if offset is None:
            offset = top[0]
            top[0] += -(-size // 32) * 32
        assert offset + size <= limit, (name, offset, size, limit)
        return nc.alloc_sbuf_tensor_at(name, shape, dt, offset=offset)

    raw = [place(f"raw{s}", [P, CB, P]) for s in range(RING)]
    w_hi = [place(f"w_hi{s}", [P, CB, P], F32R) for s in range(RING)]
    w_lo = [place(f"w_lo{s}", [P, CB, P], F32R) for s in range(RING)]
    u_hi = place("u_hi", [P, KD, T], F32R)
    u_lo = place("u_lo", [P, KD, T], F32R)
    region_x = top[0]
    top[0] += 2 * KD * T * 4
    consts = place("consts", [P, N_CONST])
    mod = place("mod", [P, 6 * KD, NSEQ])
    b_ada = place("b_ada", [P, 6 * KD])
    ln = place("ln", [P, 4, KD])
    region_h = top[0]

    x = place("x", [P, KD, T], offset=region_x)
    half_x = region_x + KD * T * 4
    c_raw = place("c_raw", [P, KD, NSEQ], offset=half_x)
    c_exp = place("c_exp", [P, KD, NSEQ], offset=half_x + 640)
    w_f = place("w_f", [P, KD, H], offset=half_x + 1280)
    b_f = place("b_f", [P, H], offset=half_x + 1792)
    f_rows = place("f_rows", [H, T], offset=half_x + 2016)
    f_z = place("f_z", [P, 3, H], offset=half_x + 1824)
    f_t = place("f_t", [P, 3, H], offset=half_x + 1920)
    oa_hi = place("oa_hi", [P, H, T], F32R, offset=region_x)
    oa_lo = place("oa_lo", [P, H, T], F32R, offset=region_x + H * T * 4)
    ob_hi = place("ob_hi", [P, H, T], F32R, offset=half_x)
    ob_lo = place("ob_lo", [P, H, T], F32R, offset=half_x + H * T * 4)
    r = place("r", [P, KD, T], offset=region_x)

    def scratch(base):
        cur = [base]

        def take(name, shape, dt=F32):
            o = cur[0]
            cur[0] += -(-int(np.prod(shape[1:])) * 4 // 32) * 32
            return place(name, shape, dt, offset=o)
        return take, cur

    take, _ = scratch(half_x)
    EXT = 2 + TP + NB * (2 + TS)
    a_ext = [take(f"a_ext{q}", [P, EXT]) for q in range(2)]
    conv = [take(f"conv{q}", [P, EXT]) for q in range(2)]
    h_f = take("h_f", [P, T])
    ln_sum = take("ln_sum", [P, T])
    ln_mean = take("ln_mean", [P, T])
    ln_var = take("ln_var", [P, T])
    ln_sumsq = take("ln_sumsq", [P, T])
    warm = take("warm", [P, 1])
    ln_shift = take("ln_shift", [P, T])
    ln_sq = [take(f"ln_sq{q}", [P, T]) for q in range(2)]
    u2_f = [take(f"u2_f{q}", [P, T]) for q in range(2)]
    y_t = take("y_t", [P, T])

    take, cur = scratch(region_h)
    kv = take("kv", [P, NB * NPG, 2 * P])
    state = take("state", [P, NB, DH])
    tab = [take(f"tab{q}", [P, N_TAB]) for q in range(2)]
    v_rows = take("v_rows", [P, 3, DH])
    kr_rows = take("kr_rows", [P, 3, DH])
    vr_rows = take("vr_rows", [P, 3, DH])
    v_seq = take("v_seq", [NS, NB, DH])
    probs = take("probs", [P, 384])
    probs_t = take("probs_t", [P, 384])
    past_t = probs_t[:, 0:P]
    att = take("att", [P, 448])
    row_p = take("row_p", [NS, T])
    row_pt = take("row_pt", [P, 192])
    o_ret = take("o_ret", [P, T])
    o_cen = take("o_cen", [P, T])
    o_sq = att[:, 0:T]
    o_var = take("o_var", [P, T])
    q_dec = take("q_dec", [P, NS])
    swap = take("swap", [P, T])
    g_exp = take("g_exp", [P, T])
    state_p = take("state_p", [P, DH])
    lf_h = take("lf_h", [P, 3])
    lfp_h = take("lfp_h", [P, NB * NPG])
    smx = take("smx", [P, 4])
    srow = take("srow", [P, 4])
    ssum = take("ssum", [P, 4])
    lf = take("lf", [P, 3, H])
    lfp = take("lfp", [P, NB * NPG, H])
    c_hl = take("c_hl", [P, (KD - 1) * 2 * CROW + P], F32R)
    c_parts = c_hl[:, 0:KD * 2 * CROW].rearrange("p (k c) -> p k c", c=2 * CROW)
    ada_rows = take("ada_rows", [2 * CROW, 2 * P])
    cossin = take("cossin", [P, 2, T])
    qkv_at = cur[0] = max(cur[0], region_h + 3 * KD * T * 4 - 7 * T * 4)
    tiles = [{u: take(f"{u}{q}", [P, T]) for u in GEMMS} for q in (1, 0)][::-1]
    gate_at = qkv_at + 7 * T * 4
    gate = [place(f"gate{n}", [P, T], offset=gate_at + n * T * 4) for n in range(2 * PRE)]
    assert region_h + 3 * KD * T * 4 <= gate_at, (gate_at - region_h, 3 * KD * T * 4)
    m_hi = place("m_hi", [P, KD, T], F32R, offset=region_h)
    m_lo = place("m_lo", [P, KD, T], F32R, offset=region_h + KD * T * 4)
    x_again = place("x_again", [P, KD, T], offset=region_h + 2 * KD * T * 4)
    take, _ = scratch(region_h)
    h_hi = take("h_hi", [P, HALF, T], F32R)
    h_lo = take("h_lo", [P, HALF, T], F32R)
    w_conv = take("w_conv", [P, KF, 4])
    s_conv = take("s_conv", [P, KF, NB, 2])
    conv_out = take("conv_out", [P, KF, NSEQ, 2])
    ln_a = take("ln_a", [P, KD, NSEQ])
    ln_c = take("ln_c", [P, KD, NSEQ])

    def c_(col, n, rows=P):
        return consts[0:rows, col:col + n]

    ctx = ExitStack()
    with ctx:
        banks = [ctx.enter_context(nc.psum_tensor(f"bank{b}", [P, 512], F32)) for b in range(8)]
        ADA_BANK, MOD_BANK = banks[2], banks[7]
        ADA_BANKS = (banks[2], banks[3])
        LOGIT_BANK, LOGF_BANK = banks[5], banks[6]
        WORK = banks[3:7]

        def sem(name):
            return ctx.enter_context(nc.semaphore(name))

        landed = [sem(f"landed{s}") for s in range(RING)]
        hi_made, lo_made, used = sem("hi_made"), sem("lo_made"), sem("used")
        x_in, c_in, small_in, pages_in = sem("x_in"), sem("c_in"), sem("small_in"), sem("pages_in")
        consts_in, w_f_in = sem("consts_in"), sem("w_f_in")
        x_again_in, ffn_in = sem("x_again_in"), sem("ffn_in")
        c_exp_made, c_silu, c_hi_made, c_ready = sem("c_exp_made"), sem("c_silu"), sem("c_hi_made"), sem("c_ready")
        bias_one, ada_staged, ada_turned = sem("bias_one"), sem("ada_staged"), sem("ada_turned")
        mod_made = sem("mod_made")
        u_prompt, u_mul, u_f32 = sem("u_prompt"), sem("u_mul"), sem("u_f32")
        u_hi_made, u_lo_made = sem("u_hi_made"), sem("u_lo_made")
        f_done, f_rows_made, f_turned = sem("f_done"), sem("f_rows_made"), sem("f_turned")
        f_zero, f_z_made, f_abs, f_exp = sem("f_zero"), sem("f_z_made"), sem("f_abs"), sem("f_exp")
        f_one, f_ln, lf_ready, lf_out = sem("f_one"), sem("f_ln"), sem("lf_ready"), sem("lf_out")
        plain = sem("plain")
        swapped, rope_step, roped = sem("swapped"), sem("rope_step"), sem("roped")
        g_exp_made, g_one, g_inv, g_silu = sem("g_exp_made"), sem("g_one"), sem("g_inv"), sem("g_silu")
        kv_out = [sem("kv_out0"), sem("kv_out1")]
        k_in, v_in, state_in = sem("k_in"), sem("v_in"), sem("state_in")
        tab_in = [sem("tab_in0"), sem("tab_in1")]
        state_out, state_p_out = sem("state_out"), sem("state_p_out")
        written = [sem(f"written{w}") for w in range(4)]
        taken = [sem(f"taken{w}") for w in range(4)]
        gathered, neg_made, exp_made = sem("gathered"), sem("neg_made"), sem("exp_made")
        inv_made, probs_made = sem("inv_made"), sem("probs_made")
        row_neg_made, row_exp_made = sem("row_neg_made"), sem("row_exp_made")
        row_inv_made, row_probs_made = sem("row_inv_made"), sem("row_probs_made")
        v_seq_made = sem("v_seq_made")
        oa_hi_made = sem("oa_hi_made")
        sq_made, o_rstd, ob_step, ob_f32 = sem("sq_made"), sem("o_rstd"), sem("ob_step"), sem("ob_f32")
        ob_hi_made, ob_made = sem("ob_hi_made"), sem("ob_made")
        gate_exp, gate_one, gate_made = sem("gate_exp"), sem("gate_one"), sem("gate_made")
        branch_read, sum_made = sem("branch_read"), sem("sum_made")
        m_hi_made, m_made = sem("m_hi_made"), sem("m_made")
        proj_read, r_made = sem("proj_read"), sem("r_made")
        shift_done, shift_made, shifted = sem("shift_done"), sem("shift_made"), sem("shifted")
        squared, summed, sq_summed = sem("squared"), sem("summed"), sem("sq_summed")
        mean_done, sq_done, mean_made = sem("mean_done"), sem("sq_done"), sem("mean_made")
        var_step, deviation, centered = sem("var_step"), sem("deviation"), sem("centered")
        pool_centered, pool_normed = sem("pool_centered"), sem("pool_normed")
        rstd_made, normed, ln_factors = sem("rstd_made"), sem("normed"), sem("ln_factors")
        u2_prompt, u2_mul, u2_sample = sem("u2_prompt"), sem("u2_mul"), sem("u2_sample")
        u2_hi_made, u2_made, x1_made = sem("u2_hi_made"), sem("u2_made"), sem("x1_made")
        ext_zero, a_read, hist, kept = sem("ext_zero"), sem("a_read"), sem("hist"), sem("kept")
        conv_step, conv_made, gelu_made = sem("conv_step"), sem("conv_made"), sem("gelu_made")
        hf_made, h_hi_made, h_made = sem("hf_made"), sem("h_hi_made"), sem("h_made")
        y_made, y_out = sem("y_made"), sem("y_out")
        passed = {}

        block = ctx.enter_context(nc.Block())

        def seqs(ap):
            return ap.rearrange("p (b t) -> p b t", b=NB)

        def per_seq(ap):
            return ap.unsqueeze(2).to_broadcast([ap.shape[0], NB, TS])

        def rep(ap, n):
            return ap.unsqueeze(1).to_broadcast([ap.shape[0], n, ap.shape[1]])

        def histories(e):
            return e[:, 2 + TP:EXT].rearrange("p (b t) -> p b t", b=NB)

        def settle(eng):
            if eng not in passed:
                passed[eng] = sem(f"passed{len(passed)}")
            eng.sem_inc(passed[eng], 1)

        def is_written(eng, job, h):
            k = JOB[job]
            eng.wait_ge(written[k % 4], 4 * h + (k // 4 + 1))

        def is_taken(eng, job, h):
            k = JOB[job]
            eng.wait_ge(taken[k % 4], 4 * h + (k // 4 + 2))

        def tile_is_read(eng, name, h):
            if name in ("qr", "kr"):
                eng.wait_ge(swapped, 2 * h + (1 if name == "qr" else 2))
            elif name == "gr":
                eng.wait_ge(g_exp_made, h + 1)
            else:
                eng.wait_ge(plain, 4 * h + ("vr", "qa", "ka", "va").index(name) + 1)

        def chunk_used(eng, n):
            eng.wait_ge(used, n + 1)

        @block.sync
        def _(sp):
            def load(base, i=None, period=0, blocks=CB):
                n = at(base, i, period)
                if i is not None or n >= RING:
                    sp.wait_ge(lo_made, n - (RING - 1))
                sp.dma_start(raw[base % RING][:, 0:blocks, :],
                             a["w"][n, :, 0:blocks * P].rearrange("p (k c) -> p k c", k=blocks)
                             ).then_inc(landed[base % RING], 16)

            def stream(first, end, blocks=(CB,)):
                body = RING * len(blocks)
                with sp.Fori(0, (end - first) // body) as i:
                    for n in range(body):
                        load(first + n, i, body, blocks[n % len(blocks)])

            sp.dma_start(c_raw[:], a["c"]).then_inc(c_in, 16)
            sp.dma_start(b_ada[:], a["b_ada"]).then_inc(c_in, 16)
            for n in range(RING):
                load(n)
            sp.dma_start(consts[:, 0:N_FIRST], a["consts"][:, 0:N_FIRST]).then_inc(consts_in, 16)
            for g in range(4):
                load(RING + g)
                sp.dma_start(x[:, 4 * g:4 * g + 4, :], a["x"][:, 4 * g:4 * g + 4, :]).then_inc(x_in, 16)
            sp.dma_start(w_f[:], a["w_f"]).then_inc(w_f_in, 16)
            stream(2 * RING, HEADS0)

            def first_loads(u):
                if u == 1:
                    sp.dma_start(b_f[:], a["b_f"].partition_broadcast(P)).then_inc(small_in, 16)
                    sp.dma_start(cossin[:], a["cossin"]).then_inc(small_in, 16)
                    sp.dma_start(consts[:, N_FIRST:N_CONST], a["consts"][:, N_FIRST:N_CONST]).then_inc(small_in, 16)
                    sp.dma_start(ln[:], a["ln"]).then_inc(small_in, 16)
                if 1 <= u < 9:
                    for n in (2 * u - 2, 2 * u - 1):
                        page.append(sp.value_load(a["pages"][0:1, n:n + 1], min_val=0,
                                                  max_val=a["cache_lf"].shape[0] - 1))
                        sp.dma_start(lfp[:, n, :], a["cache_lf"][page[n], :, :]).then_inc(pages_in, 16)

            def pages_of(h, half, count, pages):
                for n in pages:
                    sp.dma_start(kv[:, n, half * P:(half + 1) * P],
                                 a["cache_kv"][page[n], h, half, :, :]).then_inc(count, 16)

            def for_next_step(u, h, q):
                if u == 6:
                    if not isinstance(h, int) or h >= 2:
                        is_taken(sp, "state1", h - 2)
                    sp.dma_start(tab[q][:], a["tab"][h, :, :]).then_inc(tab_in[q], 16)
                if u >= 7:
                    if u == 7 and (not isinstance(h, int) or h >= 1):
                        is_taken(sp, "past_scores", h - 1)
                    pages_of(h, 0, k_in, (2 * u - 14, 2 * u - 13))

            def for_attention(u, h, first):
                if u == 4:
                    if not first:
                        sp.wait_ge(state_out, h * 16)
                    sp.dma_start(state[:], a["state"][:, h, :, :].rearrange("b d e -> d b e")).then_inc(state_in, 16)
                if 5 <= u < 9:
                    if u == 5 and not first:
                        sp.wait_ge(oa_hi_made, h)
                    pages_of(h, 1, v_in, range(4 * u - 20, 4 * u - 16))

            def step(base, i, period, h, q, attention, first=False):
                for u in range(len(UNITS)):
                    for c in range(2):
                        load(base + 2 * u + c, i, period)
                    if isinstance(h, int) and h == 0:
                        first_loads(u)
                    for_next_step(u, h, q)
                    if attention:
                        for_attention(u, h - 1, first)

            page = []
            step(HEADS0, None, 0, 0, 0, False)
            step(HEADS0 + N_HEAD, None, 0, 1, 1, True, True)
            with sp.Fori(0, 3) as i:
                step(HEADS0 + 2 * N_HEAD, i, 2 * N_HEAD, i * 2 + 2, 0, True)
                step(HEADS0 + 3 * N_HEAD, i, 2 * N_HEAD, i * 2 + 3, 1, True)
            for n in range(GATES0, MERGE0):
                load(n)
                if GATES0 + 3 <= n < GATES0 + 8:
                    for_attention(n - GATES0 + 1, H - 1, False)
            for n in range(MERGE0, MERGE0 + 12):
                load(n)
            sp.wait_ge(ob_made, H)
            is_taken(sp, "attend", H - 1)
            sp.wait_ge(state_p_out, 16 * H)
            sp.wait_ge(state_out, 16 * H)
            for q in range(2):
                sp.wait_ge(kv_out[q], 32 * (H // 2))
            sp.wait_ge(lf_out, 32)
            sp.dma_start(x_again[:], a["x"]).then_inc(x_again_in, 16)
            stream(MERGE0 + 12, OUT0)
            stream(OUT0, UP0)
            for n in range(UP0, UP0 + RING):
                load(n)
            sp.wait_ge(r_made, KD)
            sp.dma_start(w_conv[:], a["w_conv"]).then_inc(ffn_in, 16)
            sp.dma_start(s_conv[:], a["s_conv"]).then_inc(ffn_in, 16)
            stream(UP0 + RING, DOWN0)
            stream(DOWN0, UP1, DOWN_BLOCKS)
            stream(UP1, DOWN1)
            stream(DOWN1, CHUNKS, DOWN_BLOCKS)
            sp.wait_ge(kept, 4 + 2 * KF)
            sp.dma_start(a["conv"], conv_out[:]).then_inc(y_out, 16)
            first = 0
            for end in (4, 8, 12, 14, 16):
                sp.wait_ge(y_made, end)
                sp.dma_start(a["y"][:, first:end, :], r[:, first:end, :]).then_inc(y_out, 16)
                first = end
            sp.wait_ge(y_out, 6 * 16)

        @block.gpsimd
        def _(pool):
            for w in range(4):
                pool.sem_inc(taken[w], 1)
            pool.sem_inc(ada_staged, 1)
            pool.sem_inc(ada_turned, 1)
            pool.sem_inc(mod_made, 2)
            pool.sem_inc(proj_read, 2)
            pool.sem_inc(a_read, 4)
            pool.sem_inc(hf_made, 4)
            pool.sem_inc(conv_made, 2)
            pool.sem_inc(kept, 4)
            nc.gpsimd.memset(c_hl[:].bitcast(F32), 0.0).then_inc(c_ready, 1)
            pool.wait_ge(x_in, 64)
            with pool.Fori(0, KD // 2) as g:
                pool.wait_ge(mod_made, g * 4 + 6)
                for q in range(2):
                    k = g * 2 + q
                    xs = seqs(x[:, k, TP:T])
                    nc.gpsimd.tensor_tensor(xs, xs, per_seq(mod[:, k + KD, 1:NSEQ]), ALU.mult).then_inc(u_mul, 1)
                    pool.wait_ge(u_mul, k + 1)
                    nc.gpsimd.tensor_tensor(xs, xs, per_seq(mod[:, k, 1:NSEQ]), ALU.add).then_inc(u_f32, 1)
                for q in range(2):
                    k = g * 2 + q
                    pool.wait_ge(u_hi_made, k + 1)
                    nc.gpsimd.tensor_tensor(u_lo[:, k, :], x[:, k, :], u_hi[:, k, :].bitcast(F32),
                                            ALU.subtract).then_inc(u_lo_made, 1)

            def rope(name, q, n):
                t = tiles[q][name]
                pool.wait_ge(swapped, n + 1)
                nc.gpsimd.tensor_tensor(t[:], t[:], cossin[:, 0, :], ALU.mult).then_inc(rope_step, 1)
                nc.gpsimd.tensor_tensor(swap[:], swap[:], cossin[:, 1, :], ALU.mult).then_inc(rope_step, 1)
                pool.wait_ge(rope_step, n * 2 + 2)
                nc.gpsimd.tensor_tensor(t[:], t[:], swap[:], ALU.add).then_inc(roped, 1)

            def products(u, h, q):
                if UNITS[u] in ("qr", "kr"):
                    rope(UNITS[u], q, 2 * h + (UNITS[u] == "kr"))
                if u == 7:
                    pool.wait_ge(g_inv, h + 1)
                    t = tiles[q]["gr"]
                    nc.gpsimd.tensor_tensor(t[:], t[:], g_exp[:], ALU.mult).then_inc(g_silu, 1)
                if u == 14:
                    pool.wait_ge(plain, 4 * h + 4)
                    settle(pool)
                    for n, name in enumerate(("ka", "va")):
                        pool.dma_start(a["kv_new"][n, h, :, :], tiles[q][name][:]).then_inc(kv_out[q], 16)

            def attention(u, h, q):
                if u == 1:
                    is_taken(pool, "vr_rows", h)
                    nc.gpsimd.tensor_tensor(v_seq[:], rep(vr_rows[0:NS, 2, :], NB),
                                            c_(C_SEQ, NB, NS).unsqueeze(2).to_broadcast([NS, NB, DH]),
                                            ALU.mult).then_inc(v_seq_made, 1)
                if u == 5:
                    is_taken(pool, "ret_state", h)
                    settle(pool)
                    pool.dma_start(a["ret_prompt"][h, :, :], state_p[:]).then_inc(state_p_out, 16)
                if u == 12:
                    is_taken(pool, "state1", h)
                    settle(pool)
                    pool.dma_start(a["ret_sample"][:, h, :, :].rearrange("b d e -> d b e"),
                                   state[:]).then_inc(state_out, 16)
                if u == 11:
                    pool.wait_ge(g_silu, h + 1)
                    is_taken(pool, "center", h)
                    nc.gpsimd.tensor_tensor(o_cen[:], o_cen[:], tiles[q]["gr"][:], ALU.mult).then_inc(ob_step, 1)
                    pool.wait_ge(ob_step, h + 1)
                    pool.wait_ge(o_rstd, h + 1)
                    nc.gpsimd.tensor_tensor(o_cen[:], o_cen[:], o_var[:], ALU.mult).then_inc(ob_f32, 1)

            def step(h, q, has_products, has_attention):
                for u in range(len(UNITS)):
                    if has_products:
                        products(u, h, q)
                    if has_attention:
                        attention(u, h - 1, 1 - q)

            pool.wait_ge(small_in, 64)
            step(0, 0, True, False)
            pool.wait_ge(lf_ready, 1)
            pool.dma_start(a["lf_prompt"].rearrange("(c p) h -> p c h", p=P), lf[:, 0:2, :]).then_inc(lf_out, 16)
            pool.dma_start(a["lf_sample"], lf[0:NS, 2, :]).then_inc(lf_out, 16)
            step(1, 1, True, True)
            with pool.Fori(0, 3) as i:
                step(i * 2 + 2, 0, True, True)
                step(i * 2 + 3, 1, True, True)
            step(8, 0, False, True)

            def sums(n):
                nc.gpsimd.memset(ln_sum[:], 0.0).then_inc(summed, 1)
                nc.gpsimd.memset(ln_sumsq[:], 0.0).then_inc(sq_summed, 1)

                def add(k, q):
                    pool.wait_ge(shifted, k + (n * KD + 1))
                    pool.wait_ge(summed, k + (n * KD + 1))
                    nc.gpsimd.tensor_tensor(ln_sum[:], ln_sum[:], r[:, k, :], ALU.add).then_inc(summed, 1)
                    pool.wait_ge(squared, k + (n * KD + 1))
                    pool.wait_ge(sq_summed, k + (n * KD + 1))
                    nc.gpsimd.tensor_tensor(ln_sumsq[:], ln_sumsq[:], ln_sq[q][:], ALU.add).then_inc(sq_summed, 1)

                with pool.Fori(0, KD // 2 - 1) as i:
                    for q in range(2):
                        add(i * 2 + q, q)
                add(KD - 2, 0)

            chunk_used(pool, OUT0 - 1)
            sums(0)
            pool.wait_ge(mod_made, 6 * KD + 2)
            scale2 = mod[:, 4 * KD:5 * KD, :]
            for dst, w in ((ln_a, 0), (ln_c, 1)):
                nc.gpsimd.tensor_tensor(dst[:], scale2, ln[:, w, :].unsqueeze(2).to_broadcast([P, KD, NSEQ]),
                                        ALU.mult).then_inc(ln_factors, 1)
            pool.wait_ge(ln_factors, 2)
            nc.gpsimd.tensor_tensor(ln_c[:], ln_c[:], mod[:, 3 * KD:4 * KD, :], ALU.add).then_inc(ln_factors, 1)
            for q in range(2):
                nc.gpsimd.memset(a_ext[q][:], 0.0).then_inc(ext_zero, 1)
            pool.wait_ge(ln_factors, 3)
            for k in range(KD):
                pool.wait_ge(normed, k // 2 + 1)
                if k >= 2:
                    pool.wait_ge(u2_made, k - 1)
                us = seqs(u2_f[k % 2][:, TP:T])
                nc.gpsimd.tensor_tensor(us, seqs(r[:, k, TP:T]), per_seq(ln_a[:, k, 1:NSEQ]),
                                        ALU.mult).then_inc(u2_mul, 1)
                pool.wait_ge(u2_mul, k + 1)
                nc.gpsimd.tensor_tensor(us, us, per_seq(ln_c[:, k, 1:NSEQ]), ALU.add).then_inc(u2_sample, 1)
            pool.wait_ge(ext_zero, 2)
            pool.wait_ge(ffn_in, 32)

            with pool.Fori(0, KF // 2) as i:
                for q in range(2):
                    n = i * 2 + q
                    pool.wait_ge(conv_made, n + 1)
                    pool.wait_ge(kept, n * 2 + 2)
                    nc.gpsimd.tensor_copy(histories(a_ext[q])[:, :, 0:2], s_conv[:, n, :, :]).then_inc(hist, 1)
                    pool.wait_ge(a_read, n * 2 + 6)
                    nc.gpsimd.tensor_copy(conv_out[:, n, 0, :], a_ext[q][:, TP:TP + 2]).then_inc(kept, 1)
                    nc.gpsimd.tensor_copy(conv_out[:, n, 1:NSEQ, :],
                                          histories(a_ext[q])[:, :, TS:TS + 2]).then_inc(kept, 1)
            sums(1)
            pool.wait_ge(mean_made, 2)
            pool.wait_ge(squared, 2 * KD)
            for k in range(NORM_ON_POOL, KD):
                nc.gpsimd.tensor_tensor(r[:, k, :], r[:, k, :], ln_mean[:], ALU.subtract).then_inc(pool_centered, 1)
            pool.wait_ge(rstd_made, 2)
            pool.wait_ge(pool_centered, KD - NORM_ON_POOL)
            for k in range(NORM_ON_POOL, KD):
                nc.gpsimd.tensor_tensor(r[:, k, :], r[:, k, :], ln_var[:], ALU.mult).then_inc(pool_normed, 1)

        @block.scalar
        def _(act):
            def split(base, i=None, period=0):
                if base >= CHUNKS:
                    return
                n, s = at(base, i, period), base % RING
                if i is not None or n >= RING:
                    act.wait_ge(used, n - (RING - 1))
                act.wait_ge(landed[s], at(16 * (base // RING + 1), i, 16 * (period // RING)))
                nc.scalar.activation(w_hi[s][:], raw[s][:], ACT.Copy).then_inc(hi_made, 1)

            def copy(out, in_, scale=1.0):
                return nc.scalar.activation(out, in_, ACT.Copy, scale=scale)

            act.wait_ge(c_in, 32)
            nc.scalar.activation(c_exp[:], c_raw[:], ACT.Exp, scale=-1.0).then_inc(c_exp_made, 1)
            for n in range(2):
                split(n)
            act.wait_ge(c_silu, 3)
            act.wait_ge(c_ready, 1)
            copy(c_parts[:, :, 0:NSEQ], c_raw[:]).then_inc(c_hi_made, 1)
            for n in range(2, RING):
                split(n)

            def add_bias(group, m):
                act.wait_ge(ada_turned, group + 2)
                for j in range(2):
                    nc.scalar.activation(mod[:, bass.ds(m + j, 1), :], MOD_BANK[:, CROW * j:CROW * j + NSEQ],
                                         ACT.Identity, bias=b_ada[:, bass.ds(m + j, 1)]).then_inc(mod_made, 1)

            def make_u_hi(g):
                for q in range(2):
                    k = g * 2 + q
                    act.wait_ge(u_prompt, k + 1)
                    act.wait_ge(u_f32, k + 1)
                    copy(u_hi[:, k, :], x[:, k, :]).then_inc(u_hi_made, 1)

            def conditioning(base, i, g, first):
                for half in range(2):
                    split(base + RING + 4 * half, i, 8)
                    split(base + RING + 4 * half + 1, i, 8)
                    if half == 1:
                        add_bias(g * 2, g * 2)
                        if not first:
                            make_u_hi(g - 1)
                    elif not first:
                        add_bias(g * 2 - 1, g * 2 + (KD - 2))
                    split(base + RING + 4 * half + 2, i, 8)
                    split(base + RING + 4 * half + 3, i, 8)

            act.wait_ge(bias_one, 2)
            conditioning(ADA0, None, 0, True)
            with act.Fori(0, KD // 2 - 1) as i:
                conditioning(ADA0 + 8, i, i + 1, False)
            add_bias(KD - 1, 2 * KD - 2)
            make_u_hi(KD // 2 - 1)

            def products(u, base, i, period, h, q):
                name = UNITS[u]
                if u in BIAS_AT:
                    j = BIAS_AT[u] - 4 * (u == 1)
                    if not (isinstance(h, int) and 4 * h + j < 0):
                        add_bias(h * 4 + (KD + j), h * 8 + (2 * KD + 2 * j))
                if name == "ada":
                    return
                g = GEMMS.index(name)
                t = tiles[q][name]
                bank = banks[(q + g) % 2]
                chunk_used(act, at(base + 1, i, period))
                if name in ("qr", "kr"):
                    scale = DH ** -0.5 if name == "kr" else 1.0
                    turned = 2 * h + (name == "kr")
                    if not (isinstance(turned, int) and turned == 0):
                        act.wait_ge(roped, turned)
                    copy(t[:], bank[:, 0:T], scale)
                    copy(swap[0:64, :], bank[64:P, 0:T], scale)
                    copy(swap[64:P, :], bank[0:64, 0:T], scale).then_inc(swapped, 1)
                elif name == "gr":
                    if not (isinstance(h, int) and h == 0):
                        act.wait_ge(g_silu, h)
                    copy(t[:], bank[:, 0:T])
                    nc.scalar.activation(g_exp[:], bank[:, 0:T], ACT.Exp, scale=-1.0).then_inc(g_exp_made, 1)
                else:
                    if name in ("ka", "va") and not (isinstance(h, int) and h < 2):
                        act.wait_ge(kv_out[q], (h - q) * 16)
                    copy(t[:], bank[:, 0:T], DH ** -0.5 if name == "qa" else 1.0).then_inc(plain, 1)

            def attention(job, h, q):
                work = WORK[JOB[job] % 4] if job in JOB else None
                done = taken[JOB[job] % 4] if job in JOB else None
                if job in JOB:
                    is_written(act, job, h)
                if job == "v_rows":
                    copy(v_rows[:, 0:2, :], work[:, 0:256].rearrange("p (c d) -> p c d", c=2))
                    copy(v_rows[0:NS, 2, :], work[0:NS, 256:384]).then_inc(done, 1)
                elif job == "vr_rows":
                    copy(vr_rows[:, 0:2, :], work[:, 0:256].rearrange("p (c d) -> p c d", c=2))
                    copy(vr_rows[0:NS, 2, :], work[0:NS, 256:384]).then_inc(done, 1)
                elif job == "past_scores":
                    copy(past_t[:], work[:, 0:P]).then_inc(done, 1)
                elif job == "exp":
                    act.wait_ge(neg_made, h + 1)
                    nc.scalar.activation(probs[:, 0:128], probs[:, 0:128], ACT.Exp, bias=smx[:, 2:3],
                                         accum_out=ssum[:, 0:1])
                    nc.scalar.activation(probs[:, 128:384], probs[:, 128:384], ACT.Exp, bias=smx[:, 3:4],
                                         accum_out=ssum[:, 1:2]).then_inc(exp_made, 1)
                elif job == "row_exp":
                    act.wait_ge(row_neg_made, h + 1)
                    nc.scalar.activation(row_p[:], row_p[:], ACT.Exp, bias=srow[0:NS, 1:2],
                                         accum_out=srow[0:NS, 2:3]).then_inc(row_exp_made, 1)
                elif job == "ret_state":
                    if not (isinstance(h, int) and h == 0):
                        act.wait_ge(state_p_out, h * 16)
                    copy(state_p[:], work[:, 0:DH]).then_inc(done, 1)
                elif job == "probs_t":
                    copy(probs_t[:], work[:, 0:384]).then_inc(done, 1)
                elif job == "ret_out":
                    copy(o_ret[:], work[:, 0:T]).then_inc(done, 1)
                elif job == "row_probs_t":
                    copy(row_pt[:, 0:128], work[:, 0:128])
                    copy(row_pt[0:NS, 128:192], work[0:NS, 128:192]).then_inc(done, 1)
                elif job == "attend":
                    copy(oa_hi[:, h, :], work[:, 0:T]).then_inc(oa_hi_made, 1)
                elif job == "center":
                    nc.scalar.activation(o_sq, work[:, 0:T], ACT.Square).then_inc(sq_made, 1)
                elif job == "variance":
                    nc.scalar.activation(o_var[:], work[:, 0:T], ACT.Sqrt, bias=c_(C_EPS, 1)).then_inc(done, 1)
                elif job == "ob_hi":
                    act.wait_ge(ob_f32, h + 1)
                    copy(ob_hi[:, h, :], o_cen[:]).then_inc(ob_hi_made, 1)

            def forget_logits():
                act.wait_ge(f_abs, 1)
                nc.scalar.activation(f_t[:], f_t[:], ACT.Exp, scale=-1.0).then_inc(f_exp, 1)
                act.wait_ge(f_one, 1)
                nc.scalar.activation(f_t[:], f_t[:], ACT.Ln).then_inc(f_ln, 1)

            def step(base, i, period, h, q, has_attention):
                for u in range(len(UNITS)):
                    for c in range(2):
                        split(base + RING + 2 * u + c, i, period)
                    products(u, base + 2 * u, i, period, h, q)
                    if u == 1 and isinstance(h, int) and h == 0:
                        forget_logits()
                    if has_attention:
                        for job in STEP_ACT.get(u, ()):
                            attention(job, h - 1, 1 - q)

            step(HEADS0, None, 0, 0, 0, False)
            step(HEADS0 + N_HEAD, None, 0, 1, 1, True)
            with act.Fori(0, 3) as i:
                step(HEADS0 + 2 * N_HEAD, i, 2 * N_HEAD, i * 2 + 2, 0, True)
                step(HEADS0 + 3 * N_HEAD, i, 2 * N_HEAD, i * 2 + 3, 1, True)

            act.wait_ge(kv_out[0], 32 * (H // 2))
            for u in range(2 * PRE):
                for c in range(2):
                    split(GATES0 + RING + 2 * u + c)
                if u == 1:
                    add_bias(3 * KD - 1, 6 * KD - 2)
                for job in LAST_ACT.get(u, ()):
                    attention(job, H - 1, (H - 1) % 2)
                chunk_used(act, GATES0 + 2 * u + 1)
                nc.scalar.activation(gate[u][:], banks[u % 2][:, 0:T], ACT.Exp, scale=-1.0).then_inc(gate_exp, 1)

            act.wait_ge(state_out, 16 * H)
            act.wait_ge(state_p_out, 16 * H)
            act.wait_ge(lf_out, 32)
            act.wait_ge(ob_made, H)
            act.wait_ge(kv_out[1], 32 * (H // 2))
            for m in range(PRE):
                for c in range(2):
                    split(BRANCH0 + RING + 2 * m + c)
                act.wait_ge(sum_made, m + 1)
                copy(m_hi[:, m, :], gate[2 * m][:]).then_inc(m_hi_made, 1)
            with act.Fori(0, (KD - PRE) // 2) as i:
                for q in range(2):
                    m = i * 2 + (PRE + q)
                    for side in range(2):
                        for c in range(2):
                            split(MERGE0 + RING + 6 * q + 2 * side + c, i, 12)
                        chunk_used(act, at(MERGE0 + 6 * q + 2 * side + 1, i, 12))
                        act.wait_ge(m_made, m - 1)
                        nc.scalar.activation(gate[2 * q + side][:], banks[side][:, 0:T], ACT.Exp,
                                             scale=-1.0).then_inc(gate_exp, 1)
                    for c in range(2):
                        split(MERGE0 + RING + 6 * q + 4 + c, i, 12)
                    act.wait_ge(sum_made, m + 1)
                    copy(m_hi[:, m, :], gate[2 * q][:]).then_inc(m_hi_made, 1)
            def square(k, q, n):
                act.wait_ge(shifted, k + (n * KD + 1))
                if not (isinstance(k, int) and k + n == 0):
                    act.wait_ge(sq_summed, k + n * KD)
                nc.scalar.activation(ln_sq[q][:], r[:, k, :], ACT.Square).then_inc(squared, 1)

            def out_tile(b, i, m, q):
                split(b + RING, i, RING)
                if not isinstance(m, int) or m >= 4:
                    square(m - 1, 1 - q, 0)
                split(b + RING + 1, i, RING)

            for m in range(4):
                out_tile(OUT0 + 2 * m, None, m, m % 2)
            for k in range(3):
                square(k, k % 2, 0)
            with act.Fori(0, KD // 2 - 2) as i:
                for q in range(2):
                    out_tile(OUT0 + 8 + 2 * q, i, i * 2 + (4 + q), q)

            def std(n):
                nc.scalar.activation(warm[:], c_(C_EPS, 1), ACT.Sqrt)
                square(KD - 1, 1, n)
                act.wait_ge(var_step, 2 * n + 2)
                nc.scalar.activation(ln_var[:], ln_var[:], ACT.Sqrt, bias=c_(C_EPS, 1)).then_inc(deviation, 1)

            std(0)
            act.wait_ge(ln_factors, 3)
            for k in range(KD):
                act.wait_ge(normed, k // 2 + 1)
                if k >= 2:
                    act.wait_ge(u2_made, k - 1)
                nc.scalar.activation(u2_f[k % 2][:, 0:TP], r[:, k, 0:TP], ACT.Identity, bias=ln_c[:, k, 0:1],
                                     scale=ln_a[:, k, 0:1]).then_inc(u2_prompt, 1)
                act.wait_ge(u2_prompt, k + 1)
                act.wait_ge(u2_sample, k + 1)
                copy(u_hi[:, k, :], u2_f[k % 2][:]).then_inc(u2_hi_made, 1)
                if k in SPLIT_AFTER:
                    split(UP0 + RING + SPLIT_AFTER[k])
            split(UP0 + RING + 2)
            split(UP0 + RING + 3)

            act.wait_ge(ext_zero, 2)

            def take_a(n, q):
                act.wait_ge(hist, n + 1)
                copy(a_ext[q][:, 2:2 + TP], banks[4 + 2 * q][:, 0:TP]).then_inc(a_read, 1)
                copy(histories(a_ext[q])[:, :, 2:], seqs(banks[4 + 2 * q][:, TP:T])).then_inc(a_read, 1)

            def gelu(n, q):
                act.wait_ge(conv_made, n + 3)
                nc.scalar.activation(conv[q][:, 0:EXT - 2], conv[q][:, 0:EXT - 2],
                                     ACT.Gelu_apprx_tanh).then_inc(gelu_made, 1)

            def make_h_hi(n, k):
                act.wait_ge(hf_made, n * 2 + 6)
                copy(h_hi[:, k, :], h_f[:]).then_inc(h_hi_made, 1)

            def up_tile(b, i, n, k, q):
                split(b + RING, i, 8)
                split(b + RING + 1, i, 8)
                chunk_used(act, at(b + 1, i, 8))
                take_a(n, q)
                split(b + RING + 2, i, 8)
                gelu(n, q)
                split(b + RING + 3, i, 8)
                make_h_hi(n, k)

            for q in range(2):
                chunk_used(act, UP0 + 4 + 2 * q)
                take_a(q, q)
                split(UP0 + 8 + 2 * q)
                gelu(q, q)
                split(UP0 + 9 + 2 * q)
                make_h_hi(q, q)
            with act.Fori(0, KD // 2) as i:
                for q in range(2):
                    up_tile(UP0 + 8 + 4 * q, i, i * 2 + (2 + q), i * 2 + (2 + q), q)
                    m = i * 2 + q
                    nc.scalar.activation(r[:, m, :], r[:, m, :], ACT.Identity, bias=ln[:, 1, bass.ds(m, 1)],
                                         scale=ln[:, 0, bass.ds(m, 1)]).then_inc(x1_made, 1)
            done = 2 + KD
            with act.Fori(0, (HALF - done) // 2) as i:
                for q in range(2):
                    up_tile(UP0 + 4 * (done + q), i, i * 2 + (done + q), i * 2 + (done + q), q)
            with act.Fori(0, N_DOWN // RING) as i:
                for n in range(RING):
                    split(DOWN0 + RING + n, i, RING)
            with act.Fori(0, HALF // 2) as i:
                for q in range(2):
                    up_tile(UP1 + 4 * q, i, i * 2 + (HALF + q), i * 2 + q, q)

            def down_turn(b, i, m):
                for j in range(4):
                    split(b + RING + 3 * j, i, 12)
                    if not isinstance(m, int) or m >= 4:
                        square(m + (j - 1), (j + 1) % 2, 1)
                    split(b + RING + 3 * j + 1, i, 12)
                    split(b + RING + 3 * j + 2, i, 12)

            down_turn(DOWN1, None, 0)
            for k in range(3):
                square(k, k % 2, 1)
            with act.Fori(0, 2) as i:
                down_turn(DOWN1 + 12, i, i * 4 + 4)
            down_turn(DOWN1 + 36, None, 12)
            std(1)
            for k in range(KD):
                if k < NORM_ON_POOL:
                    act.wait_ge(normed, KD // 2 + k // 2 + 1)
                else:
                    act.wait_ge(pool_normed, k - NORM_ON_POOL + 1)
                nc.scalar.activation(r[:, k, :], r[:, k, :], ACT.Identity, bias=ln[:, 3, k:k + 1],
                                     scale=ln[:, 2, k:k + 1]).then_inc(y_made, 1)

        @block.vector
        def _(dve):
            def split(base, i=None, period=0):
                if base >= CHUNKS:
                    return
                n, s = at(base, i, period), base % RING
                dve.wait_ge(hi_made, n + 1)
                nc.vector.tensor_tensor(w_lo[s][:], raw[s][:], w_hi[s][:].bitcast(F32),
                                        ALU.subtract).then_inc(lo_made, 1)

            dve.wait_ge(c_exp_made, 1)
            nc.vector.tensor_scalar(c_exp[:], c_exp[:], 1.0, None, ALU.add).then_inc(c_silu, 1)
            for n, m in enumerate((KD, 4 * KD)):
                nc.vector.tensor_scalar(b_ada[:, m:m + KD], b_ada[:, m:m + KD], 1.0, None, ALU.add)\
                    .then_inc(bias_one, 1)
            dve.wait_ge(c_silu, 1)
            nc.vector.reciprocal(c_exp[:], c_exp[:]).then_inc(c_silu, 1)
            dve.wait_ge(c_silu, 2)
            nc.vector.tensor_tensor(c_raw[:], c_raw[:], c_exp[:], ALU.mult).then_inc(c_silu, 1)
            for n in range(2):
                split(n)
            dve.wait_ge(c_hi_made, 1)
            nc.vector.tensor_tensor(c_parts[:, :, CROW:CROW + NSEQ], c_raw[:], c_parts[:, :, 0:NSEQ].bitcast(F32),
                                    ALU.subtract).then_inc(c_ready, 1)
            for n in range(2, RING):
                split(n)

            def stage(group, base, i=None, period=0, bank=ADA_BANK):
                chunk_used(dve, at(base, i, period))
                dve.wait_ge(ada_turned, group + 1)
                nc.vector.tensor_copy(ada_rows[:], bank[0:2 * CROW, 0:2 * P]).then_inc(ada_staged, 1)

            def make_u_prompt(g):
                dve.wait_ge(mod_made, g * 4 + 6)
                for q in range(2):
                    k = g * 2 + q
                    nc.vector.tensor_scalar(x[:, k, 0:TP], x[:, k, 0:TP], mod[:, k + KD, 0:1], mod[:, k, 0:1],
                                            ALU.mult, ALU.add).then_inc(u_prompt, 1)

            def conditioning(base, i, g, first):
                for half in range(2):
                    for c in range(3):
                        split(base + RING + 4 * half + c, i, 8)
                    stage(g * 2 + half, base + 4 * half + 3, i, 8, ADA_BANKS[half])
                    split(base + RING + 4 * half + 3, i, 8)
                    if half == 0 and not first:
                        make_u_prompt(g - 1)

            conditioning(ADA0, None, 0, True)
            dve.wait_ge(x_in, 64)
            with dve.Fori(0, KD // 2 - 1) as i:
                conditioning(ADA0 + 8, i, i + 1, False)
            make_u_prompt(KD // 2 - 1)

            def forget_logits():
                nc.vector.memset(f_z[:], 0.0).then_inc(f_zero, 1)
                dve.wait_ge(small_in, 64)
                dve.wait_ge(f_zero, 1)
                dve.wait_ge(f_turned, 1)
                nc.vector.tensor_tensor(f_z[:, 0:2, :], LOGF_BANK[:, 0:2 * H].rearrange("p (c h) -> p c h", c=2),
                                        rep(b_f[:], 2), ALU.add).then_inc(f_z_made, 1)
                nc.vector.tensor_tensor(f_z[0:NS, 2, :], LOGF_BANK[0:NS, 2 * H:3 * H], b_f[0:NS, :],
                                        ALU.add).then_inc(f_z_made, 1)
                dve.wait_ge(f_z_made, 2)
                nc.vector.scalar_tensor_tensor(out=f_t[:], in0=f_z[:], scalar=-1.0, in1=f_z[:], op0=ALU.mult,
                                               op1=ALU.max).then_inc(f_abs, 1)
                dve.wait_ge(f_exp, 1)
                nc.vector.tensor_scalar(f_t[:], f_t[:], 1.0, None, ALU.add).then_inc(f_one, 1)
                dve.wait_ge(f_ln, 1)
                nc.vector.scalar_tensor_tensor(out=lf[:], in0=f_z[:], scalar=0.0, in1=f_t[:], op0=ALU.min,
                                               op1=ALU.subtract).then_inc(lf_ready, 1)

            def products(u, base, i, period, h, q):
                if u in STAGE_AT:
                    stage(h * 4 + (KD + STAGE_AT[u]), base + 1, i, period)
                if u == 14:
                    dve.wait_ge(lf_ready, 1)
                    dve.wait_ge(pages_in, 16 * NB * NPG)
                    nc.vector.tensor_copy(lf_h[:], lf[:, :, h]).then_inc(gathered, 1)
                    nc.vector.tensor_copy(lfp_h[:], lfp[:, :, h]).then_inc(gathered, 1)
                    dve.wait_ge(tab_in[q], (h - q) * 8 + 16)
                    dve.wait_ge(roped, 2 * h + 1)
                    nc.vector.tensor_tensor(q_dec[:], tiles[q]["qr"][:, TP:T], tab[q][:, T_CROSS:T_CROSS + NS],
                                            ALU.mult).then_inc(gathered, 1)
                if u == 7:
                    dve.wait_ge(g_exp_made, h + 1)
                    nc.vector.tensor_scalar(g_exp[:], g_exp[:], 1.0, None, ALU.add).then_inc(g_one, 1)
                    dve.wait_ge(g_one, h + 1)
                    nc.vector.reciprocal(g_exp[:], g_exp[:]).then_inc(g_inv, 1)

            def attention(job, h, q):
                work = WORK[JOB[job] % 4] if job in JOB else None
                done = taken[JOB[job] % 4] if job in JOB else None
                if job in JOB:
                    is_written(dve, job, h)
                if job == "kr_rows":
                    for c in range(3):
                        n = P if c < 2 else NS
                        last = nc.vector.tensor_scalar(kr_rows[0:n, c, :], work[0:n, c * P:(c + 1) * P],
                                                       tab[q][0:n, T_KW + c:T_KW + c + 1], None, ALU.mult)
                    last.then_inc(done, 1)
                elif job == "scores":
                    settle(dve)
                    nc.vector.tensor_tensor_reduce(probs[:, 0:128], work[:, 0:128], c_(C_MASK + 128, 128), 1.0, MASKED,
                                                   ALU.add, ALU.max, smx[:, 0:1])
                    nc.vector.tensor_tensor_reduce(probs[:, 128:384], work[:, 128:384], c_(C_MASK, 256),
                                                   1.0, MASKED, ALU.add, ALU.max, smx[:, 1:2]).then_inc(done, 1)
                    is_taken(dve, "scores", h)
                    nc.vector.tensor_scalar(smx[:, 2:4], smx[:, 0:2], -1.0, None, ALU.mult).then_inc(neg_made, 1)
                elif job == "ret_scores":
                    nc.vector.tensor_tensor(att[:, 0:256], work[:, 0:256], tab[q][:, 0:256], ALU.mult)
                    nc.vector.tensor_tensor(att[:, 256:384], work[:, 256:384], tab[q][:, 0:128], ALU.mult)
                    nc.vector.tensor_tensor(att[0:NS, 384:448], work[0:NS, 384:448],
                                            tab[q][0:NS, T_SEQ:T_SEQ + NS], ALU.mult).then_inc(done, 1)
                elif job == "row_scores":
                    settle(dve)
                    nc.vector.tensor_tensor_reduce(row_p[:], work[0:NS, 0:T], c_(C_ROWMASK, T, NS), 1.0, MASKED,
                                                   ALU.add, ALU.max, srow[0:NS, 0:1]).then_inc(done, 1)
                    is_taken(dve, "row_scores", h)
                    nc.vector.tensor_scalar(srow[0:NS, 1:2], srow[0:NS, 0:1], -1.0, None,
                                            ALU.mult).then_inc(row_neg_made, 1)
                elif job == "normalise":
                    dve.wait_ge(exp_made, h + 1)
                    nc.vector.reciprocal(ssum[:, 2:4], ssum[:, 0:2]).then_inc(inv_made, 1)
                    dve.wait_ge(inv_made, h + 1)
                    nc.vector.tensor_scalar(probs[:, 0:128], probs[:, 0:128], ssum[:, 2:3], None, ALU.mult)
                    nc.vector.tensor_scalar(probs[:, 128:384], probs[:, 128:384], ssum[:, 3:4], None,
                                            ALU.mult).then_inc(probs_made, 1)
                elif job == "row_normalise":
                    dve.wait_ge(row_exp_made, h + 1)
                    nc.vector.reciprocal(srow[0:NS, 3:4], srow[0:NS, 2:3]).then_inc(row_inv_made, 1)
                    dve.wait_ge(row_inv_made, h + 1)
                    nc.vector.tensor_scalar(row_p[:], row_p[:], srow[0:NS, 3:4], None,
                                            ALU.mult).then_inc(row_probs_made, 1)
                elif job in ("state0", "state1"):
                    b = 4 * (job == "state1")
                    nc.vector.scalar_tensor_tensor(
                        out=state[:, b:b + 4, :], in0=state[:, b:b + 4, :], scalar=tab[q][:, T_DECAY:T_DECAY + 1],
                        in1=work[:].rearrange("p (b e) -> p b e", b=4), op0=ALU.mult, op1=ALU.add).then_inc(done, 1)
                elif job == "attend":
                    dve.wait_ge(oa_hi_made, h + 1)
                    nc.vector.tensor_tensor(oa_lo[:, h, :], work[:, 0:T], oa_hi[:, h, :].bitcast(F32),
                                            ALU.subtract).then_inc(done, 1)
                elif job == "center":
                    dve.wait_ge(sq_made, h + 1)
                    nc.vector.tensor_copy(o_cen[:], work[:, 0:T]).then_inc(done, 1)
                elif job == "deviation":
                    is_taken(dve, "variance", h)
                    nc.vector.reciprocal(o_var[:], o_var[:]).then_inc(o_rstd, 1)
                elif job == "ob_lo":
                    dve.wait_ge(ob_hi_made, h + 1)
                    nc.vector.tensor_tensor(ob_lo[:, h, :], o_cen[:], ob_hi[:, h, :].bitcast(F32),
                                            ALU.subtract).then_inc(ob_made, 1)

            def step(base, i, period, h, q, has_attention):
                for u in range(len(UNITS)):
                    for c in range(2):
                        split(base + RING + 2 * u + c, i, period)
                    products(u, base + 2 * u, i, period, h, q)
                    if u == 1 and isinstance(h, int) and h == 0:
                        forget_logits()
                    if has_attention:
                        for job in STEP_DVE.get(u, ()):
                            attention(job, h - 1, 1 - q)

            dve.wait_ge(f_done, 1)
            nc.vector.tensor_copy(f_rows[:], LOGIT_BANK[0:H, 0:T]).then_inc(f_rows_made, 1)
            step(HEADS0, None, 0, 0, 0, False)
            step(HEADS0 + N_HEAD, None, 0, 1, 1, True)
            with dve.Fori(0, 3) as i:
                step(HEADS0 + 2 * N_HEAD, i, 2 * N_HEAD, i * 2 + 2, 0, True)
                step(HEADS0 + 3 * N_HEAD, i, 2 * N_HEAD, i * 2 + 3, 1, True)

            def sigmoid(slot, g):
                dve.wait_ge(gate_exp, g + 1)
                nc.vector.tensor_scalar(gate[slot][:], gate[slot][:], 1.0, None, ALU.add).then_inc(gate_one, 1)
                dve.wait_ge(gate_one, g + 1)
                nc.vector.reciprocal(gate[slot][:], gate[slot][:]).then_inc(gate_made, 1)

            def branch(slot, bank, n):
                dve.wait_ge(gate_made, n + 1)
                nc.vector.tensor_tensor(gate[slot][:], bank[:, 0:T], gate[slot][:], ALU.mult).then_inc(branch_read, 1)

            def merge(slot, m):
                dve.wait_ge(branch_read, m * 2 + 2)
                nc.vector.tensor_tensor(gate[slot][:], gate[slot][:], gate[slot + 1][:], ALU.add).then_inc(sum_made, 1)

            def merge_lo(slot, m):
                dve.wait_ge(m_hi_made, m + 1)
                nc.vector.tensor_tensor(m_lo[:, m, :], gate[slot][:], m_hi[:, m, :].bitcast(F32),
                                        ALU.subtract).then_inc(m_made, 1)

            for u in range(2 * PRE):
                for c in range(2):
                    split(GATES0 + RING + 2 * u + c)
                for job in LAST_DVE.get(u, ()):
                    attention(job, H - 1, (H - 1) % 2)
                sigmoid(u, u)
            for m in range(PRE):
                split(BRANCH0 + RING + 2 * m)
                chunk_used(dve, BRANCH0 + 2 * m)
                branch(2 * m, banks[3 + 2 * (m % 2)], 2 * m)
                chunk_used(dve, BRANCH0 + 2 * m + 1)
                branch(2 * m + 1, banks[4 + 2 * (m % 2)], 2 * m + 1)
                merge(2 * m, m)
                split(BRANCH0 + RING + 2 * m + 1)
                merge_lo(2 * m, m)
            with dve.Fori(0, (KD - PRE) // 2) as i:
                for q in range(2):
                    m = i * 2 + (PRE + q)
                    b = MERGE0 + 6 * q
                    for side in range(2):
                        for c in range(2):
                            split(b + RING + 2 * side + c, i, 12)
                        sigmoid(2 * q + side, m * 2 + side)
                    split(b + RING + 4, i, 12)
                    chunk_used(dve, at(b + 4, i, 12))
                    branch(2 * q, banks[3 + 2 * q], m * 2)
                    chunk_used(dve, at(b + 5, i, 12))
                    branch(2 * q + 1, banks[4 + 2 * q], m * 2 + 1)
                    merge(2 * q, m)
                    split(b + RING + 5, i, 12)
                    merge_lo(2 * q, m)

            def gated_residual(bank, before, gates, m, n):
                if not (isinstance(n, int) and n == 0):
                    dve.wait_ge(r_made, n)
                nc.vector.tensor_scalar(y_t[:, 0:TP], bank[:, 0:TP], gates[:, m, 0:1], None, ALU.mult)
                nc.vector.tensor_tensor(seqs(y_t[:, TP:T]), seqs(bank[:, TP:T]), per_seq(gates[:, m, 1:NSEQ]),
                                        ALU.mult).then_inc(proj_read, 1)
                dve.wait_ge(proj_read, n + 3)
                nc.vector.scalar_tensor_tensor(out=r[:, m, :], in0=before[:, m, :], scalar=ALPHA, in1=y_t[:],
                                               op0=ALU.mult, op1=ALU.add).then_inc(r_made, 1)

            gate1, gate2 = mod[:, 2 * KD:3 * KD, :], mod[:, 5 * KD:6 * KD, :]
            dve.wait_ge(x_again_in, 16)
            dve.wait_ge(mod_made, 6 * KD + 2)

            def out_tile(b, i, m, q):
                for c in range(2):
                    split(b + RING + c, i, RING)
                chunk_used(dve, at(b + 1, i, RING))
                gated_residual(banks[q], x_again, gate1, m, m)

            def shift(m, n):
                if isinstance(m, int) and m < 2:
                    return
                tiles_now = (m,)
                if isinstance(m, int) and m == 2:
                    dve.wait_ge(shift_done, n + 1)
                    nc.vector.tensor_copy(ln_shift[:], banks[2][:, 0:T]).then_inc(shift_made, 1)
                    dve.wait_ge(shift_made, n + 1)
                    tiles_now = (0, 1, 2)
                for k in tiles_now:
                    dve.wait_ge(r_made, k + (2 * n * KD + 1))
                    nc.vector.tensor_tensor(r[:, k, :], r[:, k, :], ln_shift[:], ALU.subtract).then_inc(shifted, 1)

            for m in range(4):
                out_tile(OUT0 + 2 * m, None, m, m % 2)
                shift(m, 0)
            with dve.Fori(0, KD // 2 - 2) as i:
                for q in range(2):
                    out_tile(OUT0 + 8 + 2 * q, i, i * 2 + (4 + q), q)
                    shift(i * 2 + (4 + q), 0)

            def subtract_mean(g, n):
                rows = r[:, 2 * g:2 * g + 2, :]
                nc.vector.tensor_tensor(rows, rows, rep(ln_mean[:], 2), ALU.subtract).then_inc(centered, 1)

            def statistics(n):
                dve.wait_ge(mean_done, n + 1)
                nc.vector.tensor_scalar(ln_mean[:], banks[2][:, 0:T], 1.0 / KD, None, ALU.mult).then_inc(mean_made, 1)
                dve.wait_ge(mean_made, n + 1)
                nc.vector.tensor_tensor(ln_var[:], ln_mean[:], ln_mean[:], ALU.mult).then_inc(var_step, 1)
                dve.wait_ge(var_step, 2 * n + 1)
                dve.wait_ge(sq_done, n + 1)
                nc.vector.scalar_tensor_tensor(out=ln_var[:], in0=banks[3][:, 0:T], scalar=1.0 / KD, in1=ln_var[:],
                                               op0=ALU.mult, op1=ALU.subtract).then_inc(var_step, 1)
                subtract_mean(0, n)
                dve.wait_ge(deviation, n + 1)
                nc.vector.reciprocal(ln_var[:], ln_var[:]).then_inc(rstd_made, 1)

            def norm(g, n, pairs=KD // 2):
                if g < pairs - 1:
                    subtract_mean(g + 1, n)
                dve.wait_ge(rstd_made, n + 1)
                dve.wait_ge(centered, n * KD // 2 + g + 1)
                rows = r[:, 2 * g:2 * g + 2, :]
                nc.vector.tensor_tensor(rows, rows, rep(ln_var[:], 2), ALU.mult).then_inc(normed, 1)

            def u2_lo(k):
                dve.wait_ge(u2_hi_made, k + 1)
                nc.vector.tensor_tensor(u_lo[:, k, :], u2_f[k % 2][:], u_hi[:, k, :].bitcast(F32),
                                        ALU.subtract).then_inc(u2_made, 1)

            statistics(0)
            norm(0, 0)
            for k in range(KD):
                if k % 2 == 0 and k < KD - 2:
                    norm(k // 2 + 1, 0)
                u2_lo(k)
                if k in SPLIT_AFTER:
                    split(UP0 + RING + SPLIT_AFTER[k])
            split(UP0 + RING + 2)
            split(UP0 + RING + 3)
            dve.wait_ge(ffn_in, 32)

            def convolve(n, q):
                e, w = a_ext[q], EXT - 2
                dve.wait_ge(a_read, n * 2 + 6)
                dve.wait_ge(hist, n + 1)
                nc.vector.tensor_scalar(conv[q][:, 0:w], e[:, 2:2 + w], w_conv[:, n, 2:3], w_conv[:, n, 3:4],
                                        ALU.mult, ALU.add).then_inc(conv_step, 1)
                dve.wait_ge(conv_step, n * 2 + 1)
                nc.vector.scalar_tensor_tensor(out=conv[q][:, 0:w], in0=e[:, 1:1 + w], scalar=w_conv[:, n, 1:2],
                                               in1=conv[q][:, 0:w], op0=ALU.mult, op1=ALU.add).then_inc(conv_step, 1)
                dve.wait_ge(conv_step, n * 2 + 2)
                nc.vector.scalar_tensor_tensor(out=conv[q][:, 0:w], in0=e[:, 0:w], scalar=w_conv[:, n, 0:1],
                                               in1=conv[q][:, 0:w], op0=ALU.mult, op1=ALU.add).then_inc(conv_made, 1)

            def times_b(n, q):
                b_bank = banks[5 + 2 * q]
                dve.wait_ge(gelu_made, n + 1)
                nc.vector.tensor_tensor(h_f[:, 0:TP], conv[q][:, 0:TP], b_bank[:, 0:TP], ALU.mult).then_inc(hf_made, 1)
                nc.vector.tensor_tensor(seqs(h_f[:, TP:T]), histories(conv[q])[:, :, 0:TS],
                                        seqs(b_bank[:, TP:T]), ALU.mult).then_inc(hf_made, 1)

            def make_h_lo(n, k):
                dve.wait_ge(h_hi_made, n + 1)
                dve.wait_ge(hf_made, n * 2 + 6)
                nc.vector.tensor_tensor(h_lo[:, k, :], h_f[:], h_hi[:, k, :].bitcast(F32),
                                        ALU.subtract).then_inc(h_made, 1)

            def up(base, first, k0, turns):
                with dve.Fori(0, turns) as i:
                    for q in range(2):
                        n = i * 2 + (first + q)
                        b = base + 4 * q
                        split(b + RING, i, 8)
                        split(b + RING + 1, i, 8)
                        convolve(n, q)
                        split(b + RING + 2, i, 8)
                        chunk_used(dve, at(b + 3, i, 8))
                        times_b(n, q)
                        split(b + RING + 3, i, 8)
                        make_h_lo(n, i * 2 + (k0 + q))

            def down_turn(base, turn, i, half):
                b = base + 12 * turn
                for j in range(4):
                    for c in range(3):
                        split(b + RING + 3 * j + c, i, 12)
                    m = at(4 * turn + j, i, 4)
                    done = KD * (1 + half)
                    chunk_used(dve, at(b + 3 * j + 2, i, 12))
                    bank = banks[j % 2]
                    if half == 0:
                        dve.wait_ge(x1_made, KD)
                        gated_residual(bank, r, gate2, m, m + done)
                        continue
                    dve.wait_ge(r_made, m + done)
                    nc.vector.scalar_tensor_tensor(out=r[:, m, 0:TP], in0=bank[:, 0:TP], scalar=gate2[:, m, 0:1],
                                                   in1=r[:, m, 0:TP], op0=ALU.mult, op1=ALU.add)
                    nc.vector.tensor_tensor(seqs(y_t[:, TP:T]), seqs(bank[:, TP:T]), per_seq(gate2[:, m, 1:NSEQ]),
                                            ALU.mult).then_inc(proj_read, 1)
                    dve.wait_ge(proj_read, m + (done + 3))
                    nc.vector.tensor_tensor(r[:, m, TP:T], r[:, m, TP:T], y_t[:, TP:T], ALU.add).then_inc(r_made, 1)
                    shift(m, 1)

            for q in range(2):
                convolve(q, q)
                split(UP0 + 8 + 2 * q)
                chunk_used(dve, UP0 + 5 + 2 * q)
                times_b(q, q)
                split(UP0 + 9 + 2 * q)
                make_h_lo(q, q)
            up(UP0 + 8, 2, 2, HALF // 2 - 1)
            with dve.Fori(0, KD // 4) as i:
                down_turn(DOWN0, 0, i, 0)
            up(UP1, HALF, 0, HALF // 2)
            down_turn(DOWN1, 0, None, 1)
            with dve.Fori(0, 2) as i:
                down_turn(DOWN1, 1, i, 1)
            down_turn(DOWN1, 3, None, 1)
            statistics(1)
            for g in range(NORM_ON_POOL // 2):
                norm(g, 1, NORM_ON_POOL // 2)

        @block.tensor
        def _(pe):
            ident = c_(C_IDENT, P)

            def mm(out, lhsT, rhs, start=False, stop=False):
                return nc.tensor.matmul(out, lhsT, rhs, start=start, stop=stop, skip_group_check=True)

            def chunk(out, x_hi, x_lo, k0, base, i=None, period=0, blocks=CB, first=False, last=False,
                      ready=None, all_ready=None, between=None):
                s = base % RING
                pe.wait_ge(lo_made, at(base + 1, i, period))
                for b in range(blocks):
                    k = k0 + b
                    if ready is not None:
                        pe.wait_ge(ready, k + 1)
                    if all_ready is not None and b == blocks - 1:
                        pe.wait_ge(*all_ready)
                    mm(out, w_hi[s][:, b, :], x_lo[:, k, :], start=first and b == 0)
                    mm(out, w_hi[s][:, b, :], x_hi[:, k, :])
                    ins = mm(out, w_lo[s][:, b, :], x_hi[:, k, :], stop=last and b == blocks - 1)
                    if b == blocks - 1:
                        ins.then_inc(used, 1)
                    if between is not None:
                        between(k)

            def tile(out, x_hi, x_lo, base, i=None, period=0, all_ready=None, between=None):
                chunk(out, x_hi, x_lo, 0, base, i, period, first=True, between=between)
                chunk(out, x_hi, x_lo, CB, base + 1, i, period, last=True, all_ready=all_ready, between=between)

            def ada(c, base, i, period, group, bank=ADA_BANK, free=0):
                if c == 0 and not (isinstance(group, int) and group < free):
                    pe.wait_ge(ada_staged, group + (1 - free))
                s = base % RING
                pe.wait_ge(lo_made, at(base + 1, i, period))
                for b in range(CB // 2):
                    k = c * (CB // 2) + b
                    rows = c_hl[:, k * 2 * CROW:k * 2 * CROW + P]
                    for w in (w_hi, w_lo):
                        ins = mm(bank[:, 0:2 * P], rows, w[s][:, 2 * b:2 * b + 2, :].rearrange("p k c -> p (k c)"),
                                 start=k == 0 and w is w_hi, stop=k == KD - 1 and w is w_lo)
                ins.then_inc(used, 1)

            def turn(group):
                pe.wait_ge(ada_staged, group + 2)
                pe.wait_ge(mod_made, group * 2 + 2)
                for j in range(2):
                    ins = mm(MOD_BANK[:, CROW * j:CROW * j + NSEQ], ada_rows[:, j * P:(j + 1) * P],
                             c_(C_SUM, NSEQ, 2 * CROW), start=True, stop=True)
                ins.then_inc(ada_turned, 1)

            def logits(k):
                pe.wait_ge(u_prompt, k + 1)
                pe.wait_ge(u_f32, k + 1)
                return mm(LOGIT_BANK[0:H, 0:T], w_f[:, k, :], x[:, k, :], start=k == 0, stop=k == KD - 1)

            def conditioning(base, i, g, first=False, logits_after={}):
                for half in range(2):
                    for c in range(4):
                        ada(c, base + 4 * half + c, i, 8, g * 2 + half, ADA_BANKS[half], 1)
                        if c == 0 and first and half == 1:
                            pe.wait_ge(consts_in, 16)
                        if c == 0 and not (first and half == 0):
                            turn(g * 2 + (half - 1))
                        if 4 * half + c in logits_after:
                            logits(logits_after[4 * half + c])

            pe.wait_ge(c_ready, 2)
            conditioning(ADA0, None, 0, True)
            with pe.Fori(0, KD // 2 - 3) as i:
                conditioning(ADA0 + 8, i, i + 1)
            pe.wait_ge(w_f_in, 16)
            conditioning(HEADS0 - 16, None, KD // 2 - 2, logits_after={c: c for c in range(8)})
            conditioning(HEADS0 - 8, None, KD // 2 - 1, logits_after={1: 8, 3: 9, 5: 10, 7: 11})
            logits(KD - 4)
            logits(KD - 3)
            turn(KD - 1)
            logits(KD - 2)
            ins = logits(KD - 1)
            ins.then_inc(f_done, 1)
            pe.wait_ge(u_lo_made, KD)

            def turn_logits():
                pe.wait_ge(small_in, 64)
                pe.wait_ge(f_rows_made, 1)
                for c in range(3):
                    n = P if c < 2 else NS
                    ins = mm(LOGF_BANK[0:n, c * H:(c + 1) * H], f_rows[:, c * P:c * P + n], c_(C_IDENT, H, H),
                             start=True, stop=True)
                ins.then_inc(f_turned, 1)

            def attention(job, h, q):
                kk = JOB[job]
                w = WORK[kk % 4]
                t = tiles[q]
                pe.wait_ge(taken[kk % 4], 4 * h + (kk // 4 + 1))
                if job in ("v_rows", "kr_rows", "vr_rows"):
                    if job == "v_rows":
                        tile_is_read(pe, "va", h)
                    if job == "kr_rows":
                        pe.wait_ge(roped, 2 * h + 2)
                    src = t[{"v_rows": "va", "kr_rows": "kr", "vr_rows": "vr"}[job]]
                    for c in range(3):
                        n = P if c < 2 else NS
                        ins = nc.tensor.transpose(w[0:n, c * P:(c + 1) * P], src[:, c * P:c * P + n], ident)
                elif job == "scores":
                    pe.wait_ge(gathered, 3 * h + 3)
                    lf0, lf1 = (lf_h[:, c:c + 1].to_broadcast([P, P]) for c in range(2))
                    mm(w[:, 0:128], t["qa"][:, 0:128], t["ka"][:, 0:128], start=True)
                    mm(w[:, 0:128], lf0, c_(C_NEGTRI, 128))
                    mm(w[:, 128:384], t["qa"][:, 128:256], t["ka"][:, 0:256])
                    mm(w[:, 128:384], lf0, c_(C_NEGTRI, 256))
                    ins = mm(w[:, 256:384], lf1, c_(C_NEGTRI, 128), stop=True)
                elif job == "ret_scores":
                    mm(w[:, 0:256], t["kr"][:, 0:128], t["qr"][:, 0:256], start=True)
                    mm(w[:, 256:384], t["kr"][:, 128:256], t["qr"][:, 128:256])
                    ins = mm(w[0:NS, 384:448], t["kr"][:, TP:T], t["qr"][:, TP:T], stop=True)
                elif job == "row_scores":
                    is_taken(pe, "past_scores", h)
                    settle(pe)
                    for g in range(NPG):
                        nc.tensor.transpose(w[0:NS, g * P:(g + 1) * P], past_t[:, g * NS:(g + 1) * NS], ident)
                    mm(w[0:NS, TP:T], t["qa"][:, TP:T], t["ka"][:, TP:T], start=True)
                    ins = mm(w[0:NS, TP:T], lf_h[0:NS, 2:3].to_broadcast([NS, NS]), c_(C_NEGTRI_SEQ, NS, NS),
                             stop=True)
                elif job == "ret_state":
                    is_taken(pe, "kr_rows", h)
                    is_taken(pe, "vr_rows", h)
                    mm(w[:, 0:DH], kr_rows[:, 0, :], vr_rows[:, 0, :], start=True)
                    ins = mm(w[:, 0:DH], kr_rows[:, 1, :], vr_rows[:, 1, :], stop=True)
                elif job == "probs_t":
                    pe.wait_ge(probs_made, h + 1)
                    for c in range(3):
                        ins = nc.tensor.transpose(w[:, c * P:(c + 1) * P], probs[:, c * P:(c + 1) * P], ident)
                elif job == "row_probs_t":
                    pe.wait_ge(row_probs_made, h + 1)
                    settle(pe)
                    for g in range(NPG):
                        nc.tensor.transpose(w[:, g * NS:(g + 1) * NS], row_p[:, g * P:(g + 1) * P],
                                            c_(C_IDENT, NS, NS))
                    ins = nc.tensor.transpose(w[0:NS, 128:192], row_p[:, TP:T], c_(C_IDENT, NS, NS))
                elif job in ("state0", "state1"):
                    pe.wait_ge(v_seq_made, h + 1)
                    b = 4 * (job == "state1")
                    ins = mm(w[:].rearrange("p (b e) -> p b e", b=4), kr_rows[0:NS, 2, :], v_seq[:, b:b + 4, :],
                             start=True, stop=True)
                elif job == "center":
                    is_taken(pe, "ret_out", h)
                    ins = mm(w[:, 0:T], c_(C_CENTER, P), o_ret[:], start=True, stop=True)
                elif job == "variance":
                    pe.wait_ge(sq_made, h + 1)
                    ins = mm(w[:, 0:T], c_(C_MEAN, P), o_sq, start=True, stop=True)
                ins.then_inc(written[kk % 4], 1)

            def attention_part(job, k, h, q):
                kk = JOB[job]
                w = WORK[kk % 4]
                t = tiles[q]
                if k == 0:
                    pe.wait_ge(taken[kk % 4], 4 * h + (kk // 4 + 1))
                ins = None
                if job == "past_scores":
                    sides = [w[:, g * NS:(g + 1) * NS].rearrange("p (b t) -> p b t", b=NB) for g in range(NPG)]
                    if k == 0:
                        pe.wait_ge(k_in, (h + 1) * (16 * NB * NPG))
                        past = lfp_h[:].rearrange("p (b g) -> p g b", g=NPG)
                        mm(sides[0], c_(C_AFTER, P), per_seq(past[:, 0, :]), start=True)
                        mm(sides[0], c_(C_ONE, 1).to_broadcast([P, P]), per_seq(past[:, 1, :]))
                        mm(sides[1], c_(C_AFTER, P), per_seq(past[:, 1, :]))
                    b, g = k // NPG, k % NPG
                    ins = mm(sides[g][:, b, :], kv[:, k, 0:P], t["qa"][:, TP + b * TS:TP + (b + 1) * TS], stop=k == 15)
                elif job == "ret_out":
                    if k == 0:
                        is_taken(pe, "ret_scores", h)
                        pe.wait_ge(state_in, (h + 1) * 16)
                        mm(w[:, 0:256], vr_rows[:, 0, :], att[:, 0:256], start=True)
                        mm(w[:, 128:256], vr_rows[:, 1, :], att[:, 256:384])
                        mm(w[:, TP:T], vr_rows[0:NS, 2, :], att[0:NS, 384:448])
                    if k % 2 == 1:
                        b = k // 2
                        ins = mm(w[:, TP + b * TS:TP + (b + 1) * TS], state[:, b, :], q_dec[:, b * TS:(b + 1) * TS],
                                 stop=k == 15)
                elif job == "attend":
                    if k == 0:
                        is_taken(pe, "probs_t", h)
                        is_taken(pe, "row_probs_t", h)
                        is_taken(pe, "v_rows", h)
                        pe.wait_ge(v_in, (h + 1) * (16 * NB * NPG))
                        mm(w[:, 0:256], v_rows[:, 0, :], probs_t[:, 0:256], start=True)
                        mm(w[:, 128:256], v_rows[:, 1, :], probs_t[:, 256:384])
                        mm(w[:, TP:T], v_rows[0:NS, 2, :], row_pt[0:NS, 128:192])
                    g, b = k // NB, k % NB
                    ins = mm(w[:, TP + b * TS:TP + (b + 1) * TS], kv[:, b * NPG + g, P:2 * P],
                             row_pt[:, g * NS + b * TS:g * NS + (b + 1) * TS], stop=k == 15)
                if k == 15:
                    ins.then_inc(written[kk % 4], 1)

            def step(base, i, period, h, q, has_attention):
                for u, name in enumerate(UNITS):
                    b = base + 2 * u
                    if name == "ada":
                        n_ada = sum(x == "ada" for x in UNITS[:u])
                        for c in range(2):
                            ada(2 * (n_ada % 2) + c, b + c, i, period, h * 4 + (KD + n_ada // 2))
                    else:
                        g = GEMMS.index(name)
                        if g >= 2:
                            tile_is_read(pe, GEMMS[g - 2], h)
                        elif not (isinstance(h, int) and h == 0):
                            tile_is_read(pe, GEMMS[g + 5], h - 1)
                        between = None
                        if has_attention and u in WITHIN:
                            between = lambda k, job=WITHIN[u]: attention_part(job, k, h - 1, 1 - q)
                        tile(banks[(q + g) % 2][:, 0:T], u_hi, u_lo, b, i, period, between=between)
                    if u in TURN_AT:
                        j = TURN_AT[u] - 4 * (u == 0)
                        if not (isinstance(h, int) and 4 * h + j < 0):
                            turn(h * 4 + (KD + j))
                    if u == 0 and isinstance(h, int) and h == 0:
                        turn_logits()
                    if has_attention:
                        for job in STEP_PE.get(u, ()):
                            attention(job, h - 1, 1 - q)

            step(HEADS0, None, 0, 0, 0, False)
            step(HEADS0 + N_HEAD, None, 0, 1, 1, True)
            with pe.Fori(0, 3) as i:
                step(HEADS0 + 2 * N_HEAD, i, 2 * N_HEAD, i * 2 + 2, 0, True)
                step(HEADS0 + 3 * N_HEAD, i, 2 * N_HEAD, i * 2 + 3, 1, True)

            for u in range(2 * PRE):
                if u < 2:
                    tile_is_read(pe, GEMMS[5 + u], H - 1)
                else:
                    pe.wait_ge(gate_exp, u - 1)
                between = None
                if u in LAST_WITHIN:
                    between = lambda k, job=LAST_WITHIN[u]: attention_part(job, k, H - 1, (H - 1) % 2)
                tile(banks[u % 2][:, 0:T], u_hi, u_lo, GATES0 + 2 * u, between=between)
                if u == 0:
                    turn(3 * KD - 1)
                for job in LAST_PE.get(u, ()):
                    attention(job, H - 1, (H - 1) % 2)

            pe.wait_ge(ob_made, H)
            for w in range(4):
                pe.wait_ge(taken[w], 4 * H + 1)

            def branches(base, i, period, m, q):
                for side, (o_hi, o_lo) in enumerate(((oa_hi, oa_lo), (ob_hi, ob_lo))):
                    if not isinstance(m, int) or m >= 2:
                        pe.wait_ge(branch_read, m * 2 + (side - 3))
                    chunk(banks[3 + 2 * q + side][:, 0:T], o_hi, o_lo, 0, base + side, i, period,
                          first=True, last=True)

            for m in range(PRE):
                branches(BRANCH0 + 2 * m, None, 0, m, m % 2)
            with pe.Fori(0, (KD - PRE) // 2) as i:
                for q in range(2):
                    m = i * 2 + (PRE + q)
                    for side in range(2):
                        pe.wait_ge(gate_exp, m * 2 + (side - 1))
                        tile(banks[side][:, 0:T], u_hi, u_lo, MERGE0 + 6 * q + 2 * side, i, 12)
                    branches(MERGE0 + 6 * q + 4, i, 12, m, q)

            pe.wait_ge(m_made, KD - 1)
            pe.wait_ge(gate_exp, 2 * KD)
            def shift_sum(n):
                pe.wait_ge(r_made, 2 * n * KD + 1)
                mm(banks[2][:, 0:T], c_(C_MEAN, P), r[:, 0, :], start=True, stop=True).then_inc(shift_done, 1)

            for m in range(2):
                pe.wait_ge(proj_read, m + 1)
                tile(banks[m][:, 0:T], m_hi, m_lo, OUT0 + 2 * m, all_ready=(m_made, KD))
            shift_sum(0)
            with pe.Fori(0, KD // 2 - 1) as i:
                for q in range(2):
                    pe.wait_ge(proj_read, i * 2 + (q + 3))
                    tile(banks[q][:, 0:T], m_hi, m_lo, OUT0 + 4 + 2 * q, i, RING)

            def layer_norm(n):
                pe.wait_ge(summed, (n + 1) * KD)
                mm(banks[2][:, 0:T], c_(C_MEAN, P), ln_sum[:], start=True)
                pe.wait_ge(sq_summed, (n + 1) * KD)
                mm(banks[3][:, 0:T], c_(C_MEAN, P), ln_sumsq[:], start=True)
                pe.wait_ge(shifted, (n + 1) * KD)
                mm(banks[2][:, 0:T], c_(C_MEAN, P), r[:, KD - 1, :], stop=True).then_inc(mean_done, 1)
                pe.wait_ge(squared, (n + 1) * KD)
                mm(banks[3][:, 0:T], c_(C_MEAN, P), ln_sq[1][:], stop=True).then_inc(sq_done, 1)

            layer_norm(0)
            pe.wait_ge(branch_read, 2 * KD)

            def up(base, first, turns):
                with pe.Fori(0, turns) as i:
                    for q in range(2):
                        n = i * 2 + (first + q)
                        b = base + 4 * q
                        pe.wait_ge(a_read, n * 2 + 2)
                        tile(banks[4 + 2 * q][:, 0:T], u_hi, u_lo, b, i, 8)
                        pe.wait_ge(hf_made, n * 2 + 2)
                        tile(banks[5 + 2 * q][:, 0:T], u_hi, u_lo, b + 2, i, 8)

            def down_tile(base, i, j, half):
                pe.wait_ge(proj_read, at(j + KD * (1 + half) + 1, i, 4))
                k0 = 0
                for c, blocks in enumerate(DOWN_BLOCKS):
                    chunk(banks[j % 2][:, 0:T], h_hi, h_lo, k0, base + 3 * (j % 4) + c, i, 12, blocks,
                          first=c == 0, last=c == 2, all_ready=(h_made, HALF * (1 + half)) if c == 2 else None)
                    k0 += blocks

            pe.wait_ge(lo_made, UP0 + RING)
            for n in range(KEEP_WARM):
                mm(banks[0][:, 0:T], w_hi[0][:, 0, :], m_hi[:, 0, :], start=True, stop=True)
            for k in range(CB):
                pe.wait_ge(u2_made, k + 1)
                for t in range(4):
                    out = banks[4 + t][:, 0:T]
                    mm(out, w_hi[t][:, k, :], u_lo[:, k, :], start=k == 0)
                    mm(out, w_hi[t][:, k, :], u_hi[:, k, :])
                    ins = mm(out, w_lo[t][:, k, :], u_hi[:, k, :])
                    if k == CB - 1:
                        ins.then_inc(used, 1)
            for t in range(4):
                chunk(banks[4 + t][:, 0:T], u_hi, u_lo, CB, UP0 + RING + t, last=True,
                      ready=u2_made if t == 0 else None)
            up(UP0 + 8, 2, HALF // 2 - 1)
            pe.wait_ge(h_made, HALF - 1)
            with pe.Fori(0, KD // 4) as i:
                for j in range(4):
                    down_tile(DOWN0, i, j, 0)
            up(UP1, HALF, HALF // 2)
            pe.wait_ge(h_made, 2 * HALF - 1)
            for j in range(4):
                down_tile(DOWN1, None, j, 1)
                if j == 1:
                    shift_sum(1)
            with pe.Fori(0, KD // 4 - 1) as i:
                for j in range(4):
                    down_tile(DOWN1 + 12, i, 4 + j, 1)
            layer_norm(1)


def tables():
    j, s = np.arange(P)[:, None], np.arange(P)[None, :]
    f = np.zeros((P, N_CONST), np.float32)
    f[:, C_IDENT:C_IDENT + P] = np.eye(P)
    f[:, C_CENTER:C_CENTER + P] = np.eye(P) - 1.0 / P
    f[:, C_MEAN:C_MEAN + P] = 1.0 / P
    f[:, C_AFTER:C_AFTER + P] = j > s
    f[:, C_NEGTRI:C_NEGTRI + P] = -1.0 * (j <= s)
    f[:, C_NEGTRI + P:C_NEGTRI + 2 * P] = -1.0
    f[:, C_MASK + P:C_MASK + 2 * P] = np.where(s <= j, 0.0, MASKED)
    n = np.arange(NS)
    same = n[:, None] // TS == n[None, :] // TS
    f[:NS, C_ROWMASK + TP:C_ROWMASK + T] = np.where(same & (n[None, :] <= n[:, None]), 0.0, MASKED)
    f[:NS, C_NEGTRI_SEQ:C_NEGTRI_SEQ + NS] = -1.0 * (same & (n[:, None] <= n[None, :]))
    f[:NS, C_SEQ:C_SEQ + NB] = n[:, None] // TS == np.arange(NB)[None, :]
    f[:, C_EPS], f[:, C_ONE] = EPS, 1.0
    r = np.arange(2 * CROW)[:, None]
    f[:2 * CROW, C_SUM:C_SUM + NSEQ] = r % CROW == np.arange(NSEQ)[None, :]
    t = np.zeros((H, P, N_TAB), np.float32)
    for h in range(H):
        g = 1.0 - 2.0 ** (-5.0 - h)
        i = np.arange(TP)[None, :]
        t[h, :, 0:TP] = np.where(i >= j, g ** np.maximum(i - j, 0).astype(np.float64), 0.0)
        t[h, :NS, T_SEQ:T_SEQ + NS] = np.where(same & (n[None, :] >= n[:, None]),
                                               g ** np.maximum(n[None, :] - n[:, None], 0).astype(np.float64), 0.0)
        t[h, :, T_CROSS:T_CROSS + NS] = g ** (n % TS + 1.0)[None, :]
        t[h, :, T_KW] = g ** (TP - 1.0 - np.arange(P))
        t[h, :, T_KW + 1] = g ** (P - 1.0 - np.arange(P))
        t[h, :, T_KW + 2] = g ** (TS - 1.0 - np.arange(P) % TS)
        t[h, :, T_DECAY] = g ** TS
    half = DH // 2
    inv = (10000.0 ** (-np.arange(half, dtype=np.float32) / half)).astype(np.float32)
    pos = np.concatenate([np.arange(TP), NPG * PAGE + np.tile(np.arange(TS), NB)]).astype(np.float32)
    ang = (inv[:, None] * pos[None, :]).astype(np.float32)
    cs = np.zeros((P, 2, T), np.float32)
    cs[:half, 0], cs[half:, 0] = np.cos(ang), np.cos(ang)
    cs[:half, 1], cs[half:, 1] = -np.sin(ang), np.sin(ang)
    return f, t, cs


def by_tile(w, n_tiles):
    k = w.shape[0]
    t = w.reshape(k // CW, CB, P, n_tiles, P).transpose(3, 0, 2, 1, 4)
    return t.reshape(n_tiles, k // CW, P, CW)


def by_feature(v, n):
    return np.ascontiguousarray(np.swapaxes(v.reshape((n, P) + v.shape[1:]), 0, 1))


def weight_stream(w_ada, w_in, w_pa, w_pb, w_o, w_up, w_down):
    w = np.zeros((CHUNKS, P, CW), np.float32)
    ada = w_ada.reshape(N_GROUP, CB // 2, P, 3 * KD, 2 * P).transpose(3, 0, 2, 1, 4).reshape(3 * KD, N_GROUP, P, CW)
    w[ADA0:HEADS0] = np.stack([ada[0:KD // 2], ada[KD // 2:KD]], 1).reshape(-1, P, CW)
    rest = ada[KD:].reshape(-1, 2, P, CW)
    edges = {"qa": 0, "ka": 1024, "va": 2048, "qr": 3080, "kr": 4104, "vr": 5128, "gr": 6152}
    inp = {u: by_tile(w_in[:, c:c + H * DH], H) for u, c in edges.items()}
    gates = [by_tile(w_in[:, c:c + D], KD) for c in (7176, 7176 + D)]
    n, m = HEADS0, 0
    for h in range(H):
        for u in UNITS:
            if u == "ada":
                w[n:n + 2] = rest[m]
                m += 1
            else:
                w[n:n + 2] = inp[u][h]
            n += 2
    branch = [by_tile(w_pa, KD), by_tile(w_pb, KD)]
    for m in range(PRE):
        for side in range(2):
            w[n:n + 2] = gates[side][m]
            n += 2
    for m in range(PRE):
        for side in range(2):
            w[n] = branch[side][m, 0]
            n += 1
    for m in range(PRE, KD):
        for side in range(2):
            w[n:n + 2] = gates[side][m]
            n += 2
        for side in range(2):
            w[n] = branch[side][m, 0]
            n += 1
    w[OUT0:UP0] = by_tile(w_o, KD).reshape(-1, P, CW)
    up = by_tile(w_up, 2 * KF)
    both = np.stack([up[:KF], up[KF:]], 1)
    down = w_down.reshape(2, HALF, P, KD, P).transpose(0, 3, 2, 1, 4).reshape(2, KD, P, HALF * P)
    for half, (u0, d0) in enumerate(((UP0, DOWN0), (UP1, DOWN1))):
        w[u0:u0 + N_UP] = both[half * HALF:(half + 1) * HALF].reshape(-1, P, CW)
        for c, blocks in enumerate(DOWN_BLOCKS):
            w[d0 + c:d0 + N_DOWN:3, :, 0:blocks * P] = down[half][:, :, c * CW:c * CW + blocks * P]
    w[UP0:UP0 + 8] = w[[UP0 + 2 * (n % 4) + n // 4 for n in range(8)]]
    return w


def kernel(**inputs):
    import concourse.bacc as bacc
    from concourse.bass_utils import run_bass_kernel_spmd

    v = {k: np.asarray(x) for k, x in inputs.items()}
    pool = v["cache_k"].shape[1]
    consts, tab, cossin = tables()
    kc = v["cache_k"][0].transpose(0, 2, 3, 1)
    vc = v["cache_v"][0].transpose(0, 2, 1, 3)
    arrays = {
        "w": weight_stream(*(v[n][0] for n in ("w_ada", "w_in", "w_pa", "w_pb", "w_o", "w_up", "w_down"))),
        "x": by_feature(np.concatenate([v["x_prompt"][0], v["x_sample"].reshape(NS, D)]).T, KD),
        "c": by_feature(np.concatenate([v["c_prompt"], v["c_sample"]]).T, KD),
        "b_ada": by_feature(v["b_ada"][0], 6 * KD),
        "consts": consts, "tab": tab, "cossin": cossin,
        "w_f": by_feature(v["w_in"][0][:, 3072:3072 + H], KD),
        "b_f": v["b_f"][0],
        "ln": np.stack([by_feature(v[n][0], KD) for n in ("ln1_g", "ln1_b", "ln2_g", "ln2_b")], 1),
        "pages": v["page_table"].reshape(1, NB * NPG),
        "cache_kv": np.stack([kc, vc], 2),
        "cache_lf": v["cache_logf"][0],
        "state": v["state_ret"][0],
        "w_conv": np.concatenate([by_feature(v["conv_w"][0].T, KF), by_feature(v["conv_b"][0], KF)[:, :, None]], 2),
        "s_conv": by_feature(v["state_conv"][0].transpose(2, 0, 1), KF),
    }
    outs = {"y": (P, KD, T), "kv_new": (2, H, DH, T), "lf_prompt": (TP, H), "lf_sample": (NS, H),
            "ret_prompt": (H, DH, DH), "ret_sample": (NB, H, DH, DH), "conv": (P, KF, NSEQ, 2)}
    nc = bacc.Bacc("TRN2", target_bir_lowering=False, num_devices=1)
    arrays = {f"in_{n}": np.ascontiguousarray(x) for n, x in arrays.items()}
    args = {n[3:]: nc.dram_tensor(n, x.shape, mybir.dt.from_np(x.dtype), kind="ExternalInput").ap()
            for n, x in arrays.items()}
    args |= {n: nc.dram_tensor(f"out_{n}", s, F32, kind="ExternalOutput").ap() for n, s in outs.items()}
    build(nc, args)
    got = run_bass_kernel_spmd(nc, [arrays], core_ids=[0]).results[0]
    y = got["out_y"].transpose(2, 1, 0).reshape(T, D)
    kv_new = got["out_kv_new"].transpose(0, 3, 1, 2)
    cv = got["out_conv"].transpose(2, 3, 1, 0).reshape(NSEQ, 2, DFF)
    c = np.ascontiguousarray
    return (c(y[:TP][None]), c(y[TP:].reshape(NB, TS, D)),
            c(kv_new[0, :TP][None, None]), c(kv_new[1, :TP][None, None]), c(got["out_lf_prompt"][None, None]),
            c(got["out_ret_prompt"][None, None]), c(cv[:1][None]),
            c(kv_new[0, TP:].reshape(1, NB, TS, H, DH)), c(kv_new[1, TP:].reshape(1, NB, TS, H, DH)),
            c(got["out_lf_sample"].reshape(1, NB, TS, H)), c(got["out_ret_sample"][None]), c(cv[1:][None]))
```
